# Optimizing a Trainium2 kernel written in Bass

```python
import jax, jax.numpy as jnp
from jax import lax
import numpy as np

D_MODEL = 2048
BATCH = 1
SEQ = 256
DEPTH = 1

GRID_W = 64
CTX_LEN = 256
CHUNK = 64
EPS = 1e-6
A_HEADS = 16
A_DK = 128
A_DV = 128
A_KW = A_HEADS * A_DK
A_VW = A_HEADS * A_DV
B_HEADS = 4
B_DK = 256
B_DV = 512
B_KW = B_HEADS * B_DK
B_VW = B_HEADS * B_DV
B_RANK = 16
GATE_NORMALIZER = 16.0
IN_COLS = (A_KW, A_VW, A_KW, A_KW, A_VW, B_KW, B_KW, B_VW, B_RANK, B_RANK, B_VW, D_MODEL, D_MODEL)
N_IN = sum(IN_COLS)

kernel_name = 'hgrn2_gla_parallel_prefix_dit_block'

def rms_norm(x, g):
    xf = x.astype(jnp.float32)
    y = xf * lax.rsqrt(jnp.mean(xf * xf, axis=-1, keepdims=True) + EPS)
    return (y * g.astype(jnp.float32)).astype(x.dtype)

def heads(t, n_heads):
    b, l, w = t.shape
    return t.reshape(b, l, n_heads, w // n_heads).transpose(0, 2, 1, 3)

def unheads(t):
    b, h, l, d = t.shape
    return t.transpose(0, 2, 1, 3).reshape(b, l, h * d)

def to_colmajor(t):
    b, l, w = t.shape
    rows = l // GRID_W
    return t.reshape(b, rows, GRID_W, w).transpose(0, 2, 1, 3).reshape(b, l, w)

def from_colmajor(t):
    b, l, w = t.shape
    rows = l // GRID_W
    return t.reshape(b, GRID_W, rows, w).transpose(0, 2, 1, 3).reshape(b, l, w)

def identity(t):
    return t

def chunked_gated_scan(q, k, v, log_f, s0):
    out_dtype = v.dtype
    b, h, l, dk = q.shape
    dv = v.shape[-1]
    n = l // CHUNK

    def chunks(t):
        return jnp.moveaxis(t.astype(jnp.float32).reshape(b, h, n, CHUNK, t.shape[-1]), 2, 0)

    incl = jnp.tril(jnp.ones((CHUNK, CHUNK), dtype=bool))[:, :, None]

    def step(state, inp):
        qc, kc, vc, lfc = inp
        cum = jnp.cumsum(lfc, axis=-2)
        o_inter = jnp.einsum('bhcd,bhde->bhce', qc * jnp.exp(cum), state)
        rel = cum[:, :, :, None, :] - cum[:, :, None, :, :]
        decay = jnp.exp(jnp.where(incl, rel, -jnp.inf))
        scores = jnp.einsum('bhid,bhjd,bhijd->bhij', qc, kc, decay)
        o_intra = jnp.einsum('bhij,bhje->bhie', scores, vc)
        last = cum[:, :, -1:, :]
        k_to_end = kc * jnp.exp(last - cum)
        new_state = jnp.exp(last[:, :, 0, :])[..., None] * state + jnp.einsum('bhcd,bhce->bhde', k_to_end, vc)
        return new_state, o_inter + o_intra

    s_final, o = lax.scan(step, s0.astype(jnp.float32), (chunks(q), chunks(k), chunks(v), chunks(log_f)))
    o = jnp.moveaxis(o, 0, 2).reshape(b, h, l, dv)
    return o.astype(out_dtype), s_final

def bidirectional_scan(q, k_fwd, k_bwd, v, lf_fwd, lf_bwd, s0_fwd, s0_bwd):
    o_f, s_f = chunked_gated_scan(q, k_fwd, v, lf_fwd, s0_fwd)
    o_b, s_b = chunked_gated_scan(jnp.flip(q, 2), jnp.flip(k_bwd, 2), jnp.flip(v, 2), jnp.flip(lf_bwd, 2), s0_bwd)
    return o_f + jnp.flip(o_b, 2), s_f, s_b

def group_rms_gate(o, n_heads, g, gate):
    b, l, w = o.shape
    of = o.astype(jnp.float32).reshape(b, l, n_heads, w // n_heads)
    of = of * lax.rsqrt(jnp.mean(of * of, axis=-1, keepdims=True) + EPS)
    return (of.reshape(b, l, w) * g.astype(jnp.float32)).astype(gate.dtype) * jax.nn.silu(gate)

def hybrid_mixer(h, w_in, lb, gk_w, gk_b, a_norm_g, b_norm_g, w_pa, w_pb, w_out, states, latent, with_output):
    split_at = [int(s) for s in np.cumsum(IN_COLS)[:-1]]
    (a_q, a_i, a_ff, a_fb, a_g, b_q, b_k, b_v, b_rf, b_rb, b_g, m_a, m_b) = jnp.split(
        jnp.einsum('bld,dn->bln', h, w_in), split_at, axis=-1)
    s_af0, s_ab0, s_bf0, s_bb0 = states

    lb = lb.astype(jnp.float32)
    f_f = lb[:A_KW] + (1.0 - lb[:A_KW]) * jax.nn.sigmoid(a_ff.astype(jnp.float32))
    f_b = lb[A_KW:] + (1.0 - lb[A_KW:]) * jax.nn.sigmoid(a_fb.astype(jnp.float32))
    o_a, s_af, s_ab = bidirectional_scan(
        heads(a_q, A_HEADS), heads(1.0 - f_f, A_HEADS), heads(1.0 - f_b, A_HEADS), heads(a_i, A_HEADS),
        heads(jnp.log(f_f), A_HEADS), heads(jnp.log(f_b), A_HEADS), s_af0, s_ab0)

    order, unorder = (to_colmajor, from_colmajor) if latent else (identity, identity)
    lf_bf = jax.nn.log_sigmoid(jnp.einsum('blr,rk->blk', b_rf, gk_w[0]).astype(jnp.float32)
                               + gk_b[0].astype(jnp.float32)) / GATE_NORMALIZER
    lf_bb = jax.nn.log_sigmoid(jnp.einsum('blr,rk->blk', b_rb, gk_w[1]).astype(jnp.float32)
                               + gk_b[1].astype(jnp.float32)) / GATE_NORMALIZER
    kb = heads(order(b_k), B_HEADS)
    o_b, s_bf, s_bb = bidirectional_scan(
        heads(order(b_q), B_HEADS) * (B_DK ** -0.5), kb, kb, heads(order(b_v), B_HEADS),
        heads(order(lf_bf), B_HEADS), heads(order(lf_bb), B_HEADS), s_bf0, s_bb0)
    new_states = (s_af, s_ab, s_bf, s_bb)
    if not with_output:
        return None, new_states

    o_a = group_rms_gate(unheads(o_a), A_HEADS, a_norm_g, a_g)
    o_b = group_rms_gate(unorder(unheads(o_b)), B_HEADS, b_norm_g, b_g)
    y = (jax.nn.sigmoid(m_a) * jnp.einsum('blv,vd->bld', o_a, w_pa)
         + jax.nn.sigmoid(m_b) * jnp.einsum('blv,vd->bld', o_b, w_pb))
    return jnp.einsum('bld,de->ble', y, w_out), new_states

def setup_inputs(seed: int = 0) -> dict:
    key = jax.random.key(seed)
    ks = jax.random.split(key, 20)
    f32 = jnp.float32
    nrm = lambda k, shape, s: jax.random.normal(k, shape, f32) * s
    return {
        'x': nrm(ks[0], (BATCH, SEQ, D_MODEL), 1.0),
        'c': nrm(ks[1], (BATCH, D_MODEL), 1.0),
        'ctx': nrm(ks[2], (BATCH, CTX_LEN, D_MODEL), 1.0),
        'c_ctx': nrm(ks[3], (D_MODEL,), 1.0),
        'w_ada': nrm(ks[4], (DEPTH, D_MODEL, 3 * D_MODEL), 0.5 * D_MODEL ** -0.5),
        'b_ada': nrm(ks[5], (DEPTH, 3 * D_MODEL), 0.01),
        'norm_g': 1.0 + nrm(ks[6], (DEPTH, D_MODEL), 0.1),
        'w_in': nrm(ks[7], (DEPTH, D_MODEL, N_IN), D_MODEL ** -0.5),
        'hgrn_lb_logits': nrm(ks[8], (DEPTH + 1, 2 * A_KW), 0.5),
        'gla_w_gk': nrm(ks[9], (DEPTH, 2, B_RANK, B_KW), B_RANK ** -0.5),
        'gla_b_gk': nrm(ks[10], (DEPTH, 2, B_KW), 0.1),
        'hgrn_onorm_g': 1.0 + nrm(ks[11], (DEPTH, A_VW), 0.1),
        'gla_onorm_g': 1.0 + nrm(ks[12], (DEPTH, B_VW), 0.1),
        'w_pa': nrm(ks[13], (DEPTH, A_VW, D_MODEL), A_VW ** -0.5),
        'w_pb': nrm(ks[14], (DEPTH, B_VW, D_MODEL), B_VW ** -0.5),
        'w_out': nrm(ks[15], (DEPTH, D_MODEL, D_MODEL), D_MODEL ** -0.5),
        'final_norm_g': 1.0 + nrm(ks[16], (D_MODEL,), 0.1),
    }

def reference(x, c, ctx, c_ctx, w_ada, b_ada, norm_g, w_in, hgrn_lb_logits, gla_w_gk, gla_b_gk,
              hgrn_onorm_g, gla_onorm_g, w_pa, w_pb, w_out, final_norm_g):
    b = x.shape[0]
    lower_bounds = jnp.cumsum(jax.nn.softmax(hgrn_lb_logits.astype(jnp.float32), axis=0), axis=0)
    for l in range(DEPTH):
        shift, scale, gate = jnp.split(jnp.einsum('bd,de->be', jax.nn.silu(c), w_ada[l]) + b_ada[l], 3, axis=-1)
        shift_c, scale_c, gate_c = jnp.split(jnp.einsum('d,de->e', jax.nn.silu(c_ctx), w_ada[l]) + b_ada[l], 3, axis=-1)
        params = (w_in[l], lower_bounds[l], gla_w_gk[l], gla_b_gk[l], hgrn_onorm_g[l], gla_onorm_g[l],
                  w_pa[l], w_pb[l], w_out[l])
        zero_states = (jnp.zeros((b, A_HEADS, A_DK, A_DV), jnp.float32), jnp.zeros((b, A_HEADS, A_DK, A_DV), jnp.float32),
                       jnp.zeros((b, B_HEADS, B_DK, B_DV), jnp.float32), jnp.zeros((b, B_HEADS, B_DK, B_DV), jnp.float32))
        last = l == DEPTH - 1
        h_ctx = rms_norm(ctx, norm_g[l]) * (1.0 + scale_c) + shift_c
        y_ctx, ctx_states = hybrid_mixer(h_ctx, *params, zero_states, latent=False, with_output=not last)
        h_x = rms_norm(x, norm_g[l]) * (1.0 + scale[:, None, :]) + shift[:, None, :]
        y_x, _ = hybrid_mixer(h_x, *params, ctx_states, latent=True, with_output=True)
        x = x + gate[:, None, :] * y_x
        if not last:
            ctx = ctx + gate_c * y_ctx
    return rms_norm(x, final_norm_g)


_drawn_inputs = setup_inputs


def setup_inputs(seed=0):
    import zlib

    import numpy as np

    out = dict(_drawn_inputs(seed))
    spreads = {}
    factors = {'ctx': 2.765,
     'c_ctx': 4.201,
     'b_ada': 7.567,
     'gla_w_gk': 3.548,
     'gla_b_gk': 8.0,
     'hgrn_onorm_g': 5.324,
     'gla_onorm_g': 5.276}
    for name, (base, spread) in spreads.items():
        noise = np.random.default_rng([zlib.crc32(name.encode()), seed]).standard_normal(out[name].shape)
        drawn = base * np.exp(spread * noise) if base else spread * noise
        out[name] = __import__('jax').numpy.asarray(drawn.astype(out[name].dtype))
    for name, factor in factors.items():
        out[name] = (out[name] * factor).astype(out[name].dtype)
    return out
```

```python
from contextlib import ExitStack

import concourse.bass as bass
from concourse import mybir

F32 = mybir.dt.float32
F32R = mybir.dt.float32r
U32 = mybir.dt.uint32
ALU = mybir.AluOpType
ACT = mybir.ActivationFunctionType
AX = mybir.AxisListType

P = 128
GRID_ROWS = 4
EPS = 1e-6
GATE_NORMALIZER = 16.0
RANK = 16
A_HEADS = 16
B_HEADS = 4
B_DK = 256
B_DV = 512
RING = 5
PARTS = 4
AHEAD = 2
VISITS = 2


def strided(ap, offset, dims):
    return bass.AP(tensor=ap.tensor, offset=ap.offset + offset, ap=[list(ap.ap[0])] + [list(d) for d in dims])


def to_columns(ap):
    return ap.rearrange("p (r c) -> p c r", r=GRID_ROWS)


class Phase:

    def __init__(self, name, n0, turns, per, sources, arrivals, ring):
        self.name, self.n0, self.turns, self.per, self.sources, self.ring = name, n0, turns, per, sources, ring
        self.arrivals = list(arrivals)
        self.uses = [0] * RING
        self.order = []
        for k in range(per):
            s = k % RING if ring == RING else (n0 + k) % 4
            self.order.append((s, self.uses[s]))
            self.uses[s] += 1

    def after(self):
        return [a + self.turns * u for a, u in zip(self.arrivals, self.uses)]

    def number(self, turn, k):
        return turn * self.per + (self.n0 + k)

    def raw_slot(self, k):
        return self.order[k][0]

    def arrived(self, turn, k):
        s, nth = self.order[k]
        return turn * (16 * self.uses[s]) + 16 * (self.arrivals[s] + nth + 1)

    def part_slot(self, odd, k):
        return (self.n0 + (self.per if odd else 0) + k) % PARTS


def bass_hgrn2_gla_block(nc, x, c, ctx, c_ctx, w_ada, b_ada, norm_g, w_in, lb_logits, w_gk, b_gk,
                         a_norm_g, b_norm_g, w_pa, w_pb, w_out, final_g, ident_c, masks_c, out):
    T = x.shape[1]
    TC = ctx.shape[1]
    D = x.shape[2]
    KT = D // P
    HK = KT // 2
    NT = T + TC
    TT = T // P
    CT = TC // P
    ALLT = TT + CT
    LEVELS = T.bit_length() - 1
    MASKED = LEVELS - 1
    NS = LEVELS + 1
    BW = B_HEADS * B_DK
    ADA_GROUPS = 3 * D // 512
    COL = {}
    at = 0
    for name, width in (("aq", D), ("ai", D), ("aff", D), ("afb", D), ("ag", D), ("bq", BW), ("bk", BW),
                        ("bv", D), ("rank", 2 * RANK), ("bg", D), ("ma", D), ("mb", D)):
        COL[name] = at
        at += width
    assert at == w_in.shape[2] and T == 256 and TC == 256 and KT == 16

    w_in_v = w_in.rearrange("l (p k) n -> p (l k) n", k=KT)
    w_ada_v = w_ada.rearrange("l (p k) n -> p (l k) n", k=KT)
    w_pa_v = w_pa.rearrange("l (k p) n -> p (l k) n", p=P)
    w_pb_v = w_pb.rearrange("l (k p) n -> p (l k) n", p=P)
    w_out_v = w_out.rearrange("l (k p) n -> p (l k) n", p=P)
    x_v = x.rearrange("b (t p) d -> p (b t) d", p=P)
    ctx_v = ctx.rearrange("b (t p) d -> p (b t) d", p=P)
    out_v = out.rearrange("b (t p) d -> p (b t) d", p=P)

    o_d = [nc.dram_tensor(f"{m}_scratch", (KT, P, T), F32, kind="Internal").ap() for m in ("oa", "ob")]
    mg_d = nc.dram_tensor("merge_scratch", (KT, P, 2, T), F32, kind="Internal").ap()
    gate_d = nc.dram_tensor("gate_scratch", (1, D), F32, kind="Internal").ap()

    with ExitStack() as stack:
        def sb(name, shape, dt=F32, on=stack):
            return on.enter_context(nc.sbuf_tensor(name, shape, dt))

        def ps(name):
            return stack.enter_context(nc.psum_tensor(name, [P, 512], F32))

        def sem(name):
            return stack.enter_context(nc.semaphore(name))

        ps_proj = [ps("ps_proj0"), ps("ps_proj1")]
        ps_score = [ps("ps_score0"), ps("ps_score1")]
        ps_aux = ps("ps_aux")
        ps_turn = ps("ps_turn")
        ps_o = [ps("ps_o0"), ps("ps_o1")]

        ident = sb("ident", [P, P])
        ones = sb("ones", [P, TC])
        one_col = sb("one_col", [P, 1])
        wait_mark = sb("wait_mark", [P, 1])
        eps_col = sb("eps_col", [P, 1])
        masks = sb("masks", [P, MASKED, P], U32)
        lb_cols = sb("lb_cols", [P, 2 * A_HEADS])
        oml_cols = sb("oml_cols", [P, 2 * A_HEADS])
        a_gain = sb("a_gain", [P, KT])
        b_gain = sb("b_gain", [P, KT])
        bgk_cols = sb("bgk_cols", [P, 2 * 2 * B_HEADS])
        raw = [sb(f"raw{i}", [P, HK * P]) for i in range(RING)]
        w_hi = [sb(f"w_hi{i}", [P, HK * P], F32R) for i in range(PARTS)]
        w_lo = [sb(f"w_lo{i}", [P, HK * P], F32R) for i in range(PARTS)]

        h_stack = ExitStack()
        h_hi = sb("h_hi", [P, KT, NT], F32R, h_stack)
        h_lo = sb("h_lo", [P, KT, NT], F32R, h_stack)

        s0 = ExitStack()
        xs = sb("xs", [P, ALLT, D], F32, s0)
        c_in = sb("c_in", [P, 2, KT], F32, s0)
        c_sig = sb("c_sig", [P, 2, KT], F32, s0)
        c_act = sb("c_act", [P, KT, 2], F32, s0)
        ada_rows = sb("ada_rows", [2, 3 * D], F32, s0)
        gate_b = sb("gate_b", [1, D], F32, s0)
        ada_b = sb("ada_b", [P, 2, KT], F32, s0)
        g_col = sb("g_col", [P, KT], F32, s0)
        mod = sb("mod", [P, 2, 2, KT], F32, s0)
        sq0 = sb("sq0", [P, D], F32, s0)
        ssq0 = sb("ssq0", [P, ALLT], F32, s0)
        rstd0 = sb("rstd0", [P, ALLT], F32, s0)
        h32 = [sb(f"h32_{i}", [P, NT], F32, s0) for i in range(2)]
        lg = sb("lg", [2 * A_HEADS, 2, P], F32, s0)
        lmax = sb("lmax", [2 * A_HEADS, P], F32, s0)
        lsum = sb("lsum", [2 * A_HEADS, P], F32, s0)
        lbr = sb("lbr", [2 * A_HEADS, 2, P], F32, s0)
        rows16 = sb("rows16", [16, 3, P], F32, s0)
        s0.close()

        ms = ExitStack()
        qT = [sb(f"qT{i}", [P, T], F32, ms) for i in range(2)]
        f = [sb(f"f{i}", [P, 2, NT], F32, ms) for i in range(2)]
        kk = [sb(f"kk{i}", [P, 2, NT], F32, ms) for i in range(2)]
        tail = sb("tail", [P, 2, T], F32, ms)
        QK = [sb(f"QK{i}", [P, 2, T], F32, ms) for i in range(2)]
        k_ctx = sb("k_ctx", [P, 2, TC], F32, ms)
        k_tok = [sb(f"k_tok{i}", [P, 2, CT, P], F32, ms) for i in range(2)]
        vT = sb("vT", [P, NT], F32, ms)
        v = sb("v", [P, ALLT, B_DV], F32, ms)
        S0 = sb("S0", [P, 4, B_DV], F32, ms)
        scores = [sb(f"scores{i}", [P, TT, T], F32, ms) for i in range(2)]
        q_end = [sb(f"q_end{i}", [P, 2, T], F32, ms) for i in range(2)]
        ksum = sb("ksum", [P, T], F32, ms)
        gsig = sb("gsig", [P, T], F32, ms)
        gT = sb("gT", [P, 4, T], F32, ms)
        osq = sb("osq", [P, 4, T], F32, ms)
        rstd = sb("rstd", [P, T], F32, ms)
        on = sb("on", [P, T], F32, ms)
        og = [sb(f"og{i}", [P, T], F32, ms) for i in range(2)]
        rT = sb("rT", [2 * RANK, NT], F32, ms)
        gk_s = sb("gk_s", [2 * RANK, 2, B_DK], F32, ms)
        zab = sb("zab", [P, NT], F32, ms)
        zmin = sb("zmin", [P, NT], F32, ms)
        mg = [sb(f"mg{i}", [P, T], F32, ms) for i in range(2)]
        ms.close()
        h_stack.close()

        y_hi = sb("y_hi", [P, KT, T], F32R)
        y_lo = sb("y_lo", [P, KT, T], F32R)
        o_stack = ExitStack()
        o_hi = sb("o_hi", [P, 2, KT, T], F32R, o_stack)
        o_lo = sb("o_lo", [P, 2, KT, T], F32R, o_stack)
        o_raw = [sb(f"o_raw{i}", [P, 4, T], F32, o_stack) for i in range(2)]
        mg_all = sb("mg_all", [P, KT, 2, T], F32, o_stack)
        ya = sb("ya", [P, T], F32, o_stack)
        y32 = sb("y32", [P, T], F32, o_stack)
        o_stack.close()
        z = sb("z", [P, TT, D])
        xres = sb("xres", [P, TT, D])
        fin_row = sb("fin_row", [P, D])
        gate_row = sb("gate_row", [P, D])
        zsq = sb("zsq", [P, D])
        zss = sb("zss", [P, TT])
        zr = sb("zr", [P, TT])

        c_here = sem("c_here")
        consts_here = sem("consts_here")
        x_here = sem("x_here")
        raw_here = [sem(f"raw_here{i}") for i in range(RING)]
        ada_used = sem("ada_used")
        ada_done = sem("ada_done")
        ada_read = sem("ada_read")
        c_sig_done = sem("c_sig_done")
        c_act_done = sem("c_act_done")
        memset_done = sem("memset_done")
        lb_a = sem("lb_a")
        lb_b = sem("lb_b")
        rows_ready = sem("rows_ready")
        cols_done = sem("cols_done")
        adacol_done = sem("adacol_done")
        gate_ready = sem("gate_ready")
        gate_saved = sem("gate_saved")
        ss0_done = sem("ss0_done")
        rstd0_done = sem("rstd0_done")
        xn_done = sem("xn_done")
        xT_done = sem("xT_done")
        h32_done = sem("h32_done")
        h_hi_done = sem("h_hi_done")
        h_done = sem("h_done")
        hi_done = sem("hi_done")
        lo_done = sem("lo_done")
        half_used = sem("half_used")
        proj_done = sem("proj_done")
        bank_read = [sem("bank_read0"), sem("bank_read1")]
        q_ready = sem("q_ready")
        kb_ready = sem("kb_ready")
        fsig_ready = sem("fsig_ready")
        gsig_ready = sem("gsig_ready")
        gT_done = sem("gT_done")
        kctx_ready = sem("kctx_ready")
        vT_ready = sem("vT_ready")
        turn_in = sem("turn_in")
        turn_out = sem("turn_out")
        aux_in = sem("aux_in")
        aux_out = sem("aux_out")
        qk_ready = sem("qk_ready")
        score_done = sem("score_done")
        score_read = sem("score_read")
        scores_ready = sem("scores_ready")
        q_end_ready = sem("q_end_ready")
        o_done = sem("o_done")
        o_read = sem("o_read")
        osq_ready = sem("osq_ready")
        rstd_ready = sem("rstd_ready")
        og_ready = sem("og_ready")
        og_saved = [sem("og_saved0"), sem("og_saved1")]
        sp_ready = sem("sp_ready")
        lf_ready = sem("lf_ready")
        rT_ready = sem("rT_ready")
        gk_here = sem("gk_here")
        gk_zero = sem("gk_zero")
        mg_ready = sem("mg_ready")
        mg_saved = [sem("mg_saved0"), sem("mg_saved1")]
        o_here = [sem("o_here0"), sem("o_here1")]
        o_hi_done = sem("o_hi_done")
        o_lo_done = sem("o_lo_done")
        m_here = sem("m_here")
        y32_ready = sem("y32_ready")
        y_hi_done = sem("y_hi_done")
        y_done = sem("y_done")
        rows_here = sem("rows_here")
        z_ready = sem("z_ready")
        zss_ready = sem("zss_ready")
        zr_ready = sem("zr_ready")
        final_ready = sem("final_ready")
        out_saved = sem("out_saved")

        def of_w_in(col, n=P):
            return lambda hf, i: w_in_v[:, hf * HK:(hf + 1) * HK, bass.ds(i * P + col, n)]

        def of_out(view):
            return lambda hf, i: view[:, hf * HK:(hf + 1) * HK, bass.ds(i * P, P)]

        def halves(load, scale=1, shift=0, n=P):
            return [(load, hf, scale, shift, n) for hf in range(2)]

        a_src = sum((halves(of_w_in(COL[k])) for k in ("aq", "aff", "afb", "ai", "ag")), [])
        q_k = [sum((halves(of_w_in(COL[k]), 2, d) for k in ("bq", "bk")), []) for d in range(2)]
        b_g = sum((halves(of_w_in(COL["bg"]), 4, j) for j in range(4)), [])
        b_g_now = sum((halves(of_w_in(COL["bg"]), 4, j - 4) for j in range(4)), [])
        b_v = sum((halves(of_w_in(COL["bv"]), 4, j) for j in range(4)), [])
        phases = {}
        n0, arrivals = 0, [2 * ADA_GROUPS] * 4 + [0]
        for name, turns, src, ring in (
                ("A", A_HEADS, a_src, RING),
                ("R", 1, halves(of_w_in(COL["rank"], 2 * RANK), 0, 0, 2 * RANK), 4),
                ("M", KT, halves(of_w_in(COL["ma"])) + halves(of_w_in(COL["mb"])), 4),
                ("B0", 1, q_k[0] + q_k[1] + b_v, 4),
                ("B", B_HEADS - 1, q_k[0] + b_g_now + q_k[1] + b_v, 4),
                ("B4", 1, b_g, 4),
                ("Y", KT, halves(of_out(w_pa_v)) + halves(of_out(w_pb_v)), 4),
                ("O", D // 512, [(None, k, 1, 0, 512) for k in range(KT // 2)], 4)):
            ph = Phase(name, n0, turns, len(src), src, arrivals, ring)
            phases[name] = ph
            n0 += turns * len(src)
            arrivals = ph.after()
        follows = {"A": "R", "R": "M", "M": "B0", "B0": "B", "B": "B4", "B4": None, "Y": "O", "O": None}
        B0_G0, B_G0, B4_G = 0, 1, B_HEADS - 1

        def ahead(name, turn, k, odd, last):
            ph = phases[name]
            k += AHEAD
            if k < ph.per:
                return ph, turn, k, odd
            if not last:
                return ph, turn + 1, k - ph.per, not odd
            nxt = follows[name]
            k -= ph.per
            while nxt and k >= phases[nxt].per * phases[nxt].turns:
                k -= phases[nxt].per
                nxt = follows[nxt]
            if nxt is None:
                return None
            q, r = divmod(k, phases[nxt].per)
            return phases[nxt], q, r, bool(q % 2)

        def width(ph, k):
            return ph.sources[k][4] * (2 if ph.name == "O" else HK)

        def split_hi(act, where):
            if where is None:
                return
            ph, turn, k, odd = where
            s, w, n = ph.raw_slot(k), ph.part_slot(odd, k), width(ph, k)
            act.wait_ge(raw_here[s], ph.arrived(turn, k))
            if not (ph.name == "A" and isinstance(turn, int) and ph.number(turn, k) < PARTS):
                act.wait_ge(half_used, ph.number(turn, k) - (PARTS - 1))
            act.activation(w_hi[w][:, 0:n], raw[s][:, 0:n], ACT.Copy).then_inc(hi_done, 1)

        def split_lo(dve, where):
            if where is None:
                return
            ph, turn, k, odd = where
            s, w, n = ph.raw_slot(k), ph.part_slot(odd, k), width(ph, k)
            dve.wait_ge(hi_done, ph.number(turn, k) + 1)
            dve.tensor_tensor(w_lo[w][:, 0:n], raw[s][:, 0:n], w_hi[w][:, 0:n].bitcast(F32),
                              ALU.subtract).then_inc(lo_done, 1)

        def load_half(sp, ph, turn, k):
            n = ph.number(turn, k)
            if isinstance(n, int) and n < RING:
                if n == 0:
                    sp.wait_ge(ada_used, 8 * ADA_GROUPS)
            else:
                sp.wait_ge(lo_done, n - (ph.ring - 1))
            load, hf, scale, shift, cols = ph.sources[k]
            s = ph.raw_slot(k)
            if ph.name == "O":
                dst = raw[s][:, :].rearrange("p (k n) -> p k n", k=2)
                src = w_out_v[:, 2 * hf:2 * hf + 2, bass.ds(turn * 512, 512)]
            else:
                g0 = {"B": B_G0, "B4": B4_G}.get(ph.name, 0)
                dst = raw[s][:, 0:HK * cols].rearrange("p (k n) -> p k n", k=HK)
                src = load(hf, turn * scale + (g0 * scale + shift))
            sp.dma_start(dst, src).then_inc(raw_here[s], 16)

        units = {"A": 5, "R": 1, "M": 2, "B0": 8, "B": 12, "B4": 4, "Y": 2, "O": 2}
        first_pass = {}
        m0 = 0
        for name, per in units.items():
            first_pass[name] = m0
            m0 += per * phases[name].turns

        def bank_of(name, u, odd=0):
            return (first_pass[name] + odd * units[name] + u) % 2

        def bank_free(eng, name, pair, odd, u):
            per, m = units[name], first_pass[name] + odd * units[name] + u
            step = per if name == "A" else per // 2
            eng.wait_ge(bank_read[m % 2], pair * step + (m // 2 + ADA_GROUPS // 2))

        def unit_done(eng, name, turn, u):
            eng.wait_ge(half_used, phases[name].number(turn, 2 * u + 1) + 1)

        def project(pe, name, turn, k, odd, pair, visit, tokens):
            ph = phases[name]
            u, hf = divmod(k, 2)
            bank = ps_proj[bank_of(name, u, odd)]
            slot, cols = ph.part_slot(odd, k), ph.sources[k][4]
            if visit == 0:
                if hf == 0:
                    bank_free(pe, name, pair, odd, u)
                pe.wait_ge(lo_done, ph.number(turn, k) + 1)
            n = HK // VISITS
            for j in range(visit * n, visit * n + n):
                kt = hf * HK + j
                if name == "Y":
                    r_hi, r_lo = o_hi[:, u, kt, :], o_lo[:, u, kt, :]
                else:
                    r_hi, r_lo = h_hi[:, kt, 0:tokens], h_lo[:, kt, 0:tokens]
                hi = w_hi[slot][:, j * cols:(j + 1) * cols]
                lo = w_lo[slot][:, j * cols:(j + 1) * cols]
                pe.matmul(bank[0:cols, 0:tokens], hi, r_hi, start=kt == 0, stop=False)
                pe.matmul(bank[0:cols, 0:tokens], hi, r_lo, start=False, stop=False)
                mm = pe.matmul(bank[0:cols, 0:tokens], lo, r_hi, start=False, stop=kt == KT - 1)
            if visit == VISITS - 1:
                mm.then_inc(half_used, 1)

        AUX_B, TURN_B = 2 * A_HEADS, 2 * A_HEADS

        def aux_b(g, what):
            if isinstance(g, int) and g == 0:
                return AUX_B + {"z00": 0, "z01": 1, "z10": 2, "z11": 3}[what]
            order = ["z00", "z01", "s0", "s1", "s2", "s3", "ss", "z10", "z11"]
            if isinstance(g, int) and g == B_HEADS:
                order = ["s0", "s1", "s2", "s3", "ss"]
            return g * 9 + (AUX_B + 4 - 9 + order.index(what))

        def turn_k(vh_turn, branch, d=0):
            return vh_turn * 2 + 1 if branch == "A" else vh_turn * 6 + (TURN_B + d)

        def turn_v(turn, branch, j=0):
            return turn * 2 if branch == "A" else turn * 6 + (TURN_B + 2 + j)

        def known(n, least):
            return isinstance(n, int) and n <= least

        def decay_a(dve, h, b, direction):
            dve.wait_ge(fsig_ready, h * 2 + (direction + 1))
            col = h + direction * A_HEADS
            fd = f[b][:, 1 - direction, :]
            dve.tensor_scalar(fd, fd, oml_cols[:, bass.ds(col, 1)], lb_cols[:, bass.ds(col, 1)],
                              ALU.mult, ALU.add)
            dve.drain()
            dve.tensor_scalar(kk[b][:, direction, :], fd, -1.0, 1.0, ALU.mult, ALU.add)

        def decay_b(dve, g, d, direction):
            col = g * 2 + (direction * 2 * B_HEADS + d)
            n = aux_b(g, f"z{d}{direction}")
            dve.drain()
            dve.wait_ge(sp_ready, g * 4 + (2 * d + direction + 1))
            dve.tensor_scalar(zmin[:, :], ps_aux[:, :], bgk_cols[:, bass.ds(col, 1)], 0.0,
                              ALU.add, ALU.min).then_inc(aux_out, 1)
            dve.drain()
            dve.tensor_tensor(f[d][:, 1 - direction, T:NT], zmin[:, T:NT], zab[:, T:NT], ALU.subtract)
            dve.tensor_tensor(f[d][:, 1 - direction, 0:T].rearrange("p (c r) -> p c r", r=GRID_ROWS),
                              to_columns(zmin[:, 0:T]), to_columns(zab[:, 0:T]),
                              ALU.subtract).then_inc(lf_ready, 1)

        def context_keys(dve, b, kd, waits):
            dve.drain()
            for what, count in waits:
                dve.wait_ge(what, count)
            dve.tensor_tensor_scan(k_ctx[:, 0, TC - 2::-1], f[b][:, 1, NT - 1:T:-1], ones[:, 0:TC - 1], 1.0,
                                   ALU.mult, ALU.mult)
            dve.tensor_tensor_scan(k_ctx[:, 1, 1:TC], f[b][:, 0, T:NT - 1], ones[:, 0:TC - 1], 1.0,
                                   ALU.mult, ALU.mult)
            dve.tensor_copy(strided(k_ctx[:, 0, :], TC - 1, [[1, 2]]),
                            strided(kk[b][:, 0, :], NT - 1, [[kd - (TC - 1), 2]]))
            dve.drain()
            dims = [[TC + 1, 2], [1, TC - 1]]
            dve.tensor_tensor(strided(k_ctx[:, 0, :], 0, dims), strided(k_ctx[:, 0, :], 0, dims),
                              strided(kk[b][:, 0, :], T, [[kd + 1, 2], [1, TC - 1]]), ALU.mult).then_inc(kctx_ready, 1)

        def level(dve, vh, b, kd, lv):
            s = 1 << lv
            n = T // (2 * s)
            base = vh * NS
            q0, f0, k0, t0 = qT[b][:, :], f[b][:, 0, :], kk[b][:, 0, :], tail[:, 0, :]
            if lv == 0:
                dve.drain()
                dve.wait_ge(q_ready, vh + 1)
                dve.memset(tail[:, :, :], 1.0)
                if not known(vh, 0):
                    dve.wait_ge(score_done, base)
                dve.tensor_tensor(ksum[:, :], kk[b][:, 0, 0:T], strided(k0, kd, [[1, T]]),
                                  ALU.add).then_inc(qk_ready, 1)
            if lv >= 2:
                dve.wait_ge(score_done, base + lv)
            q_out, k_out = QK[lv % 2][:, 0, :], QK[lv % 2][:, 1, :]
            pairs = [[s, 2], [2 * s, n], [1, s]]
            dve.tensor_tensor(strided(q_out, 0, pairs), strided(q0, 0, pairs),
                              strided(f0, 0, [[NT + s, 2], [2 * s, n], [1, s]]), ALU.mult)
            k_dims = [[kd + s, 2], [2 * s, n], [1, s]]
            if lv == 0:
                dve.tensor_copy(strided(k_out, 0, pairs), strided(k0, 0, k_dims)).then_inc(qk_ready, 1)
            else:
                dve.tensor_tensor(strided(k_out, 0, pairs), strided(k0, 0, k_dims),
                                  strided(t0, 0, [[T + s, 2], [2 * s, n], [1, s]]), ALU.mult).then_inc(qk_ready, 1)
            dve.drain()
            if lv < LEVELS - 1:
                t_dims = [[T + s, 2], [2 * s, n], [1, s]]
                dve.tensor_tensor(strided(t0, 0, t_dims), strided(t0, 0, t_dims),
                                  strided(f0, NT + 2 * s - 1, [[-(NT + 2 * s - 1), 2], [2 * s, n], [0, s]]), ALU.mult)
                dve.drain()
            f_dims = [[NT + s, 2], [2 * s, n], [1, s]]
            dve.tensor_tensor(strided(f0, 0, f_dims), strided(f0, 0, f_dims),
                              strided(f0, s, [[NT - 1, 2], [2 * s, n], [0, s]]), ALU.mult)
            dve.drain()

        def take_scores(dve, vh, b, i, free=None):
            if i == 0 and free is not None:
                dve.wait_ge(*free)
            dve.wait_ge(score_done, vh * NS + (i + 1))
            src = ps_score[i % 2][:, 0:T]
            blocks = strided(scores[b][:, 0, :], 0, [[T + P, 2], [1, P]])
            if i == 0:
                dve.tensor_copy(blocks, src.rearrange("p (t n) -> p t n", t=2)).then_inc(score_read, 1)
            elif i <= MASKED:
                dve.memset(wait_mark[:, :], 0.0)
                m = masks[:, i - 1, :]
                dve.copy_predicated(blocks, strided(m, 0, [[0, 2], [1, P]]),
                                    src.rearrange("p (t n) -> p t n", t=2)).then_inc(score_read, 1)
            else:
                dve.tensor_copy(strided(scores[b][:, 0, :], P, [[1, T]]), src).then_inc(score_read, 1)
            dve.drain()

        def queries_end(dve, vh, b, free):
            if free is not None:
                dve.wait_ge(*free)
            dve.tensor_tensor(q_end[b][:, :, :], strided(qT[b][:, :], 0, [[0, 2], [1, T]]),
                              strided(f[b][:, 0, :], 0, [[NT, 2], [1, T]]), ALU.mult).then_inc(q_end_ready, 1)

        def gate_silu(dve, name, turn, u, odd, n, slot):
            dve.wait_ge(gsig_ready, n + 1)
            b = bank_of(name, u, odd)
            dve.tensor_tensor(gT[:, slot, :], ps_proj[b][:, 0:T], gsig[:, :], ALU.mult).then_inc(bank_read[b], 1)
            dve.drain().then_inc(gT_done, 1)

        def gate_output(dve, src, slot, gain, rs, n, nb, saved, permuted):
            dve.drain()
            dve.wait_ge(rstd_ready, rs)
            dve.tensor_tensor(on[:, :], src, rstd[:, :], ALU.mult).then_inc(o_read, 1)
            dve.drain()
            if saved is not None:
                dve.wait_ge(og_saved[nb], saved)
            o_in, g_in, o_out = on[:, :], gT[:, slot, :], og[nb][:, :]
            if permuted:
                o_in = o_in.rearrange("p (c r) -> p r c", r=GRID_ROWS)
                g_in = g_in.rearrange("p (r c) -> p r c", r=GRID_ROWS)
                o_out = o_out.rearrange("p (r c) -> p r c", r=GRID_ROWS)
            dve.scalar_tensor_tensor(o_out, o_in, gain, g_in, ALU.mult, ALU.mult).then_inc(og_ready, 1)

        def logit_steps(act, g, d, direction):
            n = aux_b(g, f"z{d}{direction}")
            i = g * 4 + (2 * d + direction)
            col = g * 2 + (direction * 2 * B_HEADS + d)
            act.wait_ge(aux_in, n + 1)
            if not known(i, 0):
                act.wait_ge(lf_ready, i)
            act.activation(zab[:, :], ps_aux[:, :], ACT.Abs, bias=bgk_cols[:, bass.ds(col, 1)])
            act.drain()
            act.activation(zab[:, :], zab[:, :], ACT.Exp, scale=-1.0)
            act.drain()
            act.activation(zab[:, :], zab[:, :], ACT.Ln, bias=one_col[:, :]).then_inc(sp_ready, 1)

        def decay_exp(act, g, d, direction):
            act.wait_ge(lf_ready, g * 4 + (2 * d + direction + 1))
            fd = f[d][:, 1 - direction, :]
            act.activation(fd, fd, ACT.Exp, scale=1.0 / GATE_NORMALIZER).then_inc(fsig_ready, 1)

        def norm_scale(act, src, n, width, before):
            act.wait_ge(aux_in, n + 1)
            if before is not None:
                act.wait_ge(o_read, before)
            act.activation(rstd[:, :], src, ACT.Ln, bias=eps_col[:, :], scale=1.0 / width).then_inc(aux_out, 1)
            act.drain()
            act.activation(rstd[:, :], rstd[:, :], ACT.Exp, scale=-0.5).then_inc(rstd_ready, 1)

        def read_turned(act, n, dst):
            act.wait_ge(turn_in, n + 1)
            act.activation(dst, ps_turn[:, :].rearrange("p (t n) -> p t n", t=4), ACT.Copy).then_inc(turn_out, 1)

        def turn_four(pe, n, tiles, ready):
            pe.wait_ge(*ready)
            if not known(n, 0):
                pe.wait_ge(turn_out, n)
            for t, tile in enumerate(tiles):
                mm = pe.transpose(ps_turn[:, t * P:(t + 1) * P], tile, ident[:, :])
            mm.then_inc(turn_in, 1)

        def score_product(pe, vh, b, i):
            pe.wait_ge(qk_ready, vh * NS + (i + 1))
            if i < 2:
                if not known(vh, 0):
                    pe.wait_ge(score_read, vh * NS)
            else:
                pe.wait_ge(score_read, vh * NS + (i - 1))
            dst = ps_score[i % 2][:, 0:T]
            if i == 0:
                q, k = qT[b][:, :], ksum[:, :]
            else:
                q, k = QK[(i - 1) % 2][:, 0, :], QK[(i - 1) % 2][:, 1, :]
            for t in range(TT):
                tq = t if i <= MASKED else 1 - t
                mm = pe.matmul(dst[:, t * P:(t + 1) * P], k[:, t * P:(t + 1) * P], q[:, tq * P:(tq + 1) * P],
                               start=True, stop=True)
            mm.then_inc(score_done, 1)

        LEVEL_AT = [0, 1, 3, 4, 6, 7, 9, 10]
        assert len(LEVEL_AT) == LEVELS

        def scan_dve(dve, t, vh, b, kd, free):
            if t in LEVEL_AT:
                level(dve, vh, b, kd, LEVEL_AT.index(t))
            if t == 3:
                take_scores(dve, vh, b, 0, free)
            if t - 3 in LEVEL_AT:
                take_scores(dve, vh, b, LEVEL_AT.index(t - 3) + 1)
            if t == 11:
                queries_end(dve, vh, b, free)

        def scan_pe(pe, t, vh, b):
            if t == 2:
                score_product(pe, vh, b, 0)
            if t - 2 in LEVEL_AT:
                score_product(pe, vh, b, LEVEL_AT.index(t - 2) + 1)

        class Head:

            def __init__(self, pair, odd):
                self.pair, self.odd = pair, odd
                self.n = pair * 2 + odd

        A_SLOTS = 4 * 5
        A_FIRST = [Head(0, 0), Head(0, 1), Head(1, 0)]
        A_LAST = Head(A_HEADS // 2 - 1, 1)

        def heads_of(eng, body):
            body(A_FIRST[0], None, False)
            body(A_FIRST[1], A_FIRST[0], False)
            body(A_FIRST[2], A_FIRST[1], False)
            with eng.Fori(1, A_HEADS // 2 - 1) as j:
                body(Head(j, 1), Head(j, 0), False)
                body(Head(j + 1, 0), Head(j, 1), False)
            body(A_LAST, Head(A_HEADS // 2 - 1, 0), True)

        def tail_of_a(t):
            return ("R", 0, t) if t < 4 else ("M", (t - 4) // 8, (t - 4) % 8)

        def a_dve(dve, t, own, p):
            if p is not None:
                if t == 1:
                    gate_silu(dve, "A", p.n, 4, p.odd, p.n, 0)
                free = None if known(p.n, 1) else (o_done, p.n - 1)
                scan_dve(dve, t, p.n, p.odd, NT, free)
                if t == 14:
                    dve.drain().then_inc(scores_ready, 1)
                if t == 18:
                    gate_output(dve, ps_o[0][:, 0:T], 0, a_gain[:, bass.ds(p.n, 1)], p.n + 1, p.n, p.odd,
                                None if known(p.pair, 0) else p.pair * 16, False)
            if own is not None:
                if t in (9, 13):
                    decay_a(dve, own.n, own.odd, 0 if t == 9 else 1)
                if t == 14:
                    context_keys(dve, own.odd, NT, [] if known(own.n, 0) else [(turn_in, own.n * 2)])

        def a_act(act, t, own, p):
            if p is not None:
                if t == 0:
                    unit_done(act, "A", p.n, 4)
                    if not known(p.n, 0):
                        act.wait_ge(gT_done, p.n)
                    act.activation(gsig[:, :], ps_proj[bank_of("A", 4, p.odd)][:, 0:T],
                                   ACT.Sigmoid).then_inc(gsig_ready, 1)
                if t == 2:
                    act.wait_ge(aux_in, p.n * 2 + 1)
                    if not known(p.n, 0):
                        act.wait_ge(o_done, p.n)
                    act.activation(S0[:, 0:2, 0:P], ps_aux[:, 0:2 * P].rearrange("p (s n) -> p s n", s=2),
                                   ACT.Copy).then_inc(aux_out, 1)
                if t == 15:
                    act.wait_ge(o_done, p.n + 1)
                    if not known(p.n, 0):
                        act.wait_ge(aux_in, p.n * 2)
                    act.activation(osq[:, 0, :], ps_o[0][:, 0:T], ACT.Square).then_inc(osq_ready, 1)
                if t == 17:
                    norm_scale(act, ps_aux[:, 0:T], p.n * 2 + 1, P, None if known(p.n, 0) else p.n)
            if own is not None:
                if t == 4:
                    unit_done(act, "A", own.n, 0)
                    if not known(own.n, 1):
                        act.wait_ge(q_end_ready, own.n - 1)
                    b = bank_of("A", 0, own.odd)
                    act.activation(qT[own.odd][:, :], ps_proj[b][:, 0:T], ACT.Copy).then_inc(bank_read[b], 1)
                    act.drain().then_inc(q_ready, 1)
                if t in (8, 12):
                    d = 0 if t == 8 else 1
                    unit_done(act, "A", own.n, 1 + d)
                    b = bank_of("A", 1 + d, own.odd)
                    if not known(own.n, 1):
                        act.wait_ge(q_end_ready, own.n - 1)
                    act.activation(f[own.odd][:, 1 - d, :], ps_proj[b][:, :], ACT.Sigmoid).then_inc(bank_read[b], 1)
                    act.drain().then_inc(fsig_ready, 1)
                if t == 16:
                    unit_done(act, "A", own.n, 3)
                    b = bank_of("A", 3, own.odd)
                    if not known(own.n, 0):
                        act.wait_ge(turn_in, own.n * 2)
                    act.activation(vT[:, :], ps_proj[b][:, :], ACT.Copy).then_inc(bank_read[b], 1)
                    act.drain().then_inc(vT_ready, 1)
                if t == 18:
                    if not known(own.n, 0):
                        act.wait_ge(o_done, own.n)
                    read_turned(act, own.n * 2, v[:, :, 0:P])
                if t == 19:
                    read_turned(act, own.n * 2 + 1, k_tok[own.odd][:, :, :, :].rearrange("p s t n -> p (s t) n"))

        def a_pe(pe, t, own, p):
            if p is not None:
                scan_pe(pe, t, p.n, p.odd)
                if t == 1:
                    pe.wait_ge(turn_out, p.n * 2 + 2)
                    if not known(p.n, 0):
                        pe.wait_ge(aux_out, p.n * 2)
                    for s in range(2):
                        for ct in range(CT):
                            mm = pe.matmul(ps_aux[:, s * P:(s + 1) * P], k_tok[p.odd][:, 1 - s, ct, :],
                                           v[:, TT + ct, 0:P], start=ct == 0, stop=ct == CT - 1)
                    mm.then_inc(aux_in, 1)
                if t == 14:
                    pe.wait_ge(scores_ready, p.n + 1)
                    pe.wait_ge(q_end_ready, p.n + 1)
                    pe.wait_ge(aux_out, p.n * 2 + 1)
                    if not known(p.n, 0):
                        pe.wait_ge(o_read, p.n)
                    dst = ps_o[0][:, 0:T]
                    for jt in range(TT):
                        pe.matmul(dst, v[:, jt, 0:P], scores[p.odd][:, jt, :], start=jt == 0, stop=False)
                    for s in range(2):
                        mm = pe.matmul(dst, S0[:, s, 0:P], q_end[p.odd][:, s, :], start=False, stop=s == 1)
                    mm.then_inc(o_done, 1)
                if t == 16:
                    pe.wait_ge(osq_ready, p.n + 1)
                    pe.matmul(ps_aux[:, 0:T], ones[:, 0:P], osq[:, 0, :], start=True, stop=True).then_inc(aux_in, 1)
            if own is not None:
                if t == 17:
                    turn_four(pe, own.n * 2, [vT[:, i * P:(i + 1) * P] for i in range(4)], (vT_ready, own.n + 1))
                if t == 18:
                    turn_four(pe, own.n * 2 + 1, [k_ctx[:, i // CT, (i % CT) * P:(i % CT + 1) * P] for i in range(4)],
                              (kctx_ready, own.n + 1))

        VB, OB, RB = A_HEADS, A_HEADS, A_HEADS

        def b_dve(dve, t, g, d, p):
            if d == 0 and p is not None:
                if t == 14:
                    dve.tensor_tensor(scores[0][:, :, :], scores[0][:, :, :], scores[1][:, :, :],
                                      ALU.add).then_inc(scores_ready, 1)
                if t in (13, 17, 21):
                    j = (t - 13) // 4
                    gate_silu(dve, "B" if g is not None else "B4", g, (2 if g is not None else 0) + j, 0,
                              p * 4 + (OB + j), j)
                if t in (22, 23):
                    for j in ((0, 1) if t == 22 else (2,)):
                        b_out(dve, p, j)
            if d == 1 and p is not None and t == 1:
                gate_silu(dve, "B" if g is not None else "B4", g, (2 if g is not None else 0) + 3, 0,
                          p * 4 + (OB + 3), 3)
                b_out(dve, p, 3)
            if d == 0 and p is not None:
                scan_dve(dve, t, p * 2 + (VB + 1), 1, 0, (o_done, p * 4 + OB))
            if d == 1 and g is not None:
                scan_dve(dve, t, g * 2 + VB, 0, 0, (o_done, g * 4 + OB))
            if g is not None:
                if t in (1, 3):
                    decay_b(dve, g, d, t // 2)
                if t == 9:
                    before = turn_k(g, "B", 0) + (1 if d == 1 else 0 if known(g, 0) else -4)
                    waits = [(fsig_ready, g * 4 + (2 * A_HEADS + 2 * d + 2)),
                             (kb_ready, g * 2 + (d + 1)), (turn_in, before)]
                    context_keys(dve, d, 0, waits)

        def b_out(dve, p, j):
            gate_output(dve, ps_o[j % 2][:, (j // 2) * T:(j // 2) * T + T], j, b_gain[:, bass.ds(p * 4 + j, 1)],
                        p + (RB + 1), p * 4 + (OB + j), j % 2, p * 32 + (16 * (OB // 2) + 16 * (j // 2)), True)

        def b_act(act, t, g, d, p):
            if g is not None:
                if t in (1, 3):
                    logit_steps(act, g, d, t // 2)
                if t in (2, 4):
                    decay_exp(act, g, d, t // 2 - 1)
            ph = "B0" if known(g, 0) and isinstance(g, int) else "B"
            turn = 0 if ph == "B0" else (g - 1 if g is not None else None)
            u0 = 0 if d == 0 else (2 if ph == "B0" else 6)
            if g is not None:
                if t == 4:
                    unit_done(act, ph, turn, u0)
                    b = bank_of(ph, u0)
                    act.wait_ge(q_end_ready, g * 2 + (VB + d - 1))
                    act.activation(qT[d][:, :].rearrange("p (c r) -> p c r", r=GRID_ROWS),
                                   to_columns(ps_proj[b][:, 0:T]), ACT.Copy,
                                   scale=float(B_DK) ** -0.5).then_inc(bank_read[b], 1)
                    act.drain().then_inc(q_ready, 1)
                if t == 8:
                    unit_done(act, ph, turn, u0 + 1)
                    b = bank_of(ph, u0 + 1)
                    act.activation(kk[d][:, 0, 0:T].rearrange("p (c r) -> p c r", r=GRID_ROWS),
                                   to_columns(ps_proj[b][:, 0:T]), ACT.Copy)
                    act.activation(kk[d][:, 0, T:NT], ps_proj[b][:, T:NT], ACT.Copy).then_inc(bank_read[b], 1)
                    act.drain().then_inc(kb_ready, 1)
                if t == 12:
                    read_turned(act, turn_k(g, "B", d), k_tok[d][:, :, :, :].rearrange("p s t n -> p (s t) n"))
            if d == 1 and g is not None and t in (12, 16, 20):
                b_v_in(act, ph, turn, g, (t - 12) // 4)
            if d == 1 and g is not None and t in (14, 18, 22):
                b_v_out(act, g, (t - 14) // 4)
            if d == 0 and p is not None:
                if t == 0:
                    before_ph = "B0" if known(p, 0) and isinstance(p, int) else "B"
                    b_v_in(act, before_ph, 0 if before_ph == "B0" else p - 1, p, 3)
                if t == 2:
                    b_v_out(act, p, 3)
                if t in (5, 6, 7, 8):
                    act.wait_ge(aux_in, aux_b(g if g is not None else B_HEADS, f"s{t - 5}") + 1)
                    if t == 5:
                        act.wait_ge(o_done, p * 4 + OB)
                    act.activation(S0[:, t - 5, :], ps_aux[:, :], ACT.Copy).then_inc(aux_out, 1)
                if t in (12, 16, 20):
                    b_gate(act, g, p, (t - 12) // 4)
                if t in (16, 17, 18, 19):
                    j = t - 16
                    act.wait_ge(o_done, p * 4 + (OB + j + 1))
                    if j == 0:
                        act.wait_ge(rstd_ready, p + RB)
                    act.activation(osq[:, j, :], ps_o[j % 2][:, (j // 2) * T:(j // 2) * T + T],
                                   ACT.Square).then_inc(osq_ready, 1)
                if t == 21:
                    norm_scale(act, ps_aux[:, 0:T], aux_b(g if g is not None else B_HEADS, "ss"), B_DV, p * 4 + OB)
            if d == 1 and p is not None and t == 0:
                b_gate(act, g, p, 3)

        def b_v_in(act, ph, turn, g, j):
            u = (4 if ph == "B0" else 8) + j
            unit_done(act, ph, turn, u)
            b = bank_of(ph, u)
            act.wait_ge(turn_in, turn_v(g, "B", j))
            act.activation(vT[:, 0:T].rearrange("p (c r) -> p c r", r=GRID_ROWS), to_columns(ps_proj[b][:, 0:T]),
                           ACT.Copy)
            act.activation(vT[:, T:NT], ps_proj[b][:, T:NT], ACT.Copy).then_inc(bank_read[b], 1)
            act.drain().then_inc(vT_ready, 1)

        def b_v_out(act, g, j):
            if j == 0:
                act.wait_ge(o_done, g * 4 + OB)
            read_turned(act, turn_v(g, "B", j), v[:, :, j * P:(j + 1) * P])

        def b_gate(act, g, p, j):
            name, turn, u = ("B", g - 1, 2 + j) if g is not None else ("B4", 0, j)
            unit_done(act, name, turn, u)
            act.wait_ge(gT_done, p * 4 + (OB + j))
            act.activation(gsig[:, :], ps_proj[bank_of(name, u)][:, 0:T], ACT.Sigmoid).then_inc(gsig_ready, 1)

        def b_pe(pe, t, g, d, p):
            if g is not None and t in (0, 2):
                direction = t // 2
                if t == 0 and d == 0:
                    pe.wait_ge(gk_here, g * 32 + 32)
                    pe.wait_ge(rT_ready, 1)
                n = aux_b(g, f"z{d}{direction}")
                pe.wait_ge(aux_out, n)
                pe.matmul(ps_aux[:, :], gk_s[:, direction, d * P:(d + 1) * P], rT[:, :], start=True,
                          stop=True).then_inc(aux_in, 1)
            if d == 0 and p is not None:
                if t == 1:
                    turn_four(pe, turn_v(p, "B", 3), [vT[:, i * P:(i + 1) * P] for i in range(4)],
                              (vT_ready, p * 4 + (A_HEADS + 4)))
                if t in (4, 5, 6, 7):
                    s = t - 4
                    n = aux_b(g if g is not None else B_HEADS, f"s{s}")
                    if s == 0:
                        pe.wait_ge(turn_out, turn_v(p, "B", 3) + 1)
                    pe.wait_ge(aux_out, n)
                    for ct in range(CT):
                        mm = pe.matmul(ps_aux[:, :], k_tok[s // 2][:, 1 - s % 2, ct, :], v[:, TT + ct, :],
                                       start=ct == 0, stop=ct == CT - 1)
                    mm.then_inc(aux_in, 1)
                scan_pe(pe, t, p * 2 + (VB + 1), 1)
                if t in (15, 16, 17, 18):
                    j = t - 15
                    if j == 0:
                        pe.wait_ge(scores_ready, p + (RB + 1))
                        pe.wait_ge(q_end_ready, p * 2 + (VB + 2))
                        pe.wait_ge(aux_out, aux_b(g if g is not None else B_HEADS, "s3") + 1)
                        pe.wait_ge(o_read, p * 4 + OB)
                    dst = ps_o[j % 2][:, (j // 2) * T:(j // 2) * T + T]
                    if j >= 2:
                        pe.wait_ge(osq_ready, p * 4 + (OB + j - 1))
                    for jt in range(TT):
                        pe.matmul(dst, v[:, jt, j * P:(j + 1) * P], scores[0][:, jt, :], start=jt == 0, stop=False)
                    for s in range(4):
                        mm = pe.matmul(dst, S0[:, s, j * P:(j + 1) * P], q_end[s // 2][:, s % 2, :],
                                       start=False, stop=s == 3)
                    mm.then_inc(o_done, 1)
                if t == 20:
                    pe.wait_ge(osq_ready, p * 4 + (OB + 4))
                    for j in range(4):
                        mm = pe.matmul(ps_aux[:, 0:T], ones[:, 0:P], osq[:, j, :], start=j == 0, stop=j == 3)
                    mm.then_inc(aux_in, 1)
            if d == 1 and g is not None:
                scan_pe(pe, t, g * 2 + VB, 0)
                if t in (13, 17, 21):
                    j = (t - 13) // 4
                    turn_four(pe, turn_v(g, "B", j), [vT[:, i * P:(i + 1) * P] for i in range(4)],
                              (vT_ready, g * 4 + (A_HEADS + j + 1)))
            if g is not None and t == 11:
                turn_four(pe, turn_k(g, "B", d), [k_ctx[:, i // CT, (i % CT) * P:(i % CT + 1) * P] for i in range(4)],
                          (kctx_ready, g * 2 + (VB + d + 1)))

        def gla(eng, unit_slot, steps):
            def turn(ph, tn, g, p, last):
                k = 0
                for d in range(2):
                    if ph == "B4" and d == 1:
                        break
                    for t in range(24):
                        u = t // 4
                        there = {"B0": d == 1 or u < 2, "B": True, "B4": u >= 2}[ph]
                        if there:
                            wide = (u == 1) or (d == 1 and u >= 2)
                            unit_slot(ph, tn, k, t % VISITS, NT if wide else T, last)
                            k += t % VISITS == VISITS - 1
                        steps(eng, t, g, d, p)
            turn("B0", 0, 0, None, True)
            with eng.Fori(1, B_HEADS - 1) as g:
                turn("B", g - 1, g, g - 1, False)
            turn("B", B_HEADS - 2, B_HEADS - 1, B_HEADS - 2, True)
            turn("B4", 0, None, B_HEADS - 1, True)
            steps(eng, 0, None, 1, B_HEADS - 1)
            steps(eng, 1, None, 1, B_HEADS - 1)

        def merge_turns(eng, unit_slot, steps):
            for t in range(A_SLOTS):
                name, turn, s = tail_of_a(t)
                unit_slot(name, turn, s // VISITS, s % VISITS, NT if name == "R" else T, name == "R")
                steps(eng, name, turn, s, t)
            with eng.Fori(2, KT - 1) as m:
                for s in range(8):
                    unit_slot("M", m, s // VISITS, s % VISITS, T, False)
                    steps(eng, "M", m, s, None)
            for s in range(8):
                unit_slot("M", KT - 1, s // VISITS, s % VISITS, T, True)
                steps(eng, "M", KT - 1, s, None)

        block = stack.enter_context(nc.Block())

        def row_on_all(ap):
            return bass.AP(tensor=ap.tensor, offset=ap.offset, ap=[[0, P], [1, D]])

        ADA_PAIRS = ADA_GROUPS // 2

        def ada_pairs(eng, body):
            body(0)
            with eng.Fori(1, ADA_PAIRS) as i:
                body(i)

        def y_turns(eng, body):
            body(0, False)
            with eng.Fori(1, KT - 1) as i:
                body(i, False)
            body(KT - 1, True)

        Y_HALVES, O_HALVES = phases["Y"].per, phases["O"].per
        B_DONE = phases["Y"].n0

        @block.sync
        def _(sp):
            sp.dma_start(c_in[:, 0, :], c.rearrange("b (p k) -> p (b k)", k=KT)).then_inc(c_here, 16)
            sp.dma_start(c_in[:, 1, :], c_ctx.rearrange("(p k) -> p k", k=KT)).then_inc(c_here, 16)
            logits = lb_logits.rearrange("r (q p) -> q r p", p=P)
            for dst, src in ((lg[:, :, :], logits), (ident[:, :], ident_c), (masks[:, :, :], masks_c),
                             (rows16[:, 0, :], a_norm_g.rearrange("l (q p) -> (l q) p", p=P)),
                             (rows16[:, 1, :], b_norm_g.rearrange("l (q p) -> (l q) p", p=P)),
                             (rows16[:, 2, :], b_gk.rearrange("l s (q p) -> (l s q) p", p=P)),
                             (ada_b[:, 0, :], b_ada[:, 0:D].rearrange("l (p k) -> p (l k)", k=KT)),
                             (ada_b[:, 1, :], b_ada[:, D:2 * D].rearrange("l (p k) -> p (l k)", k=KT)),
                             (gate_b[:, :], b_ada[:, 2 * D:3 * D]),
                             (g_col[:, :], norm_g.rearrange("l (p k) -> p (l k)", k=KT))):
                sp.dma_start(dst, src).then_inc(consts_here, 16)
            sp.dma_start(xs[:, 0:TT, :], x_v).then_inc(x_here, 16)
            sp.dma_start(xs[:, TT:ALLT, :], ctx_v).then_inc(x_here, 16)

            def ada(i):
                for n in range(16):
                    if not (isinstance(i, int) and n < 4):
                        sp.wait_ge(ada_used, i * 16 + (n - 3))
                    g, q = divmod(n, 8)
                    sp.dma_start(raw[n % 4][:, :].rearrange("p (k n) -> p k n", k=2),
                                 w_ada_v[:, 2 * q:2 * q + 2, bass.ds(i * 1024 + g * 512, 512)]
                                 ).then_inc(raw_here[n % 4], 16)
            ada_pairs(sp, ada)

            def a_loads(own, p, last):
                for k in range(phases["A"].per):
                    load_half(sp, phases["A"], own.n, k)
            heads_of(sp, lambda own, p, last: a_loads(own, p, last))

            def visit_load(name, turn, k, visit, tokens, last):
                if visit == 0:
                    load_half(sp, phases[name], turn, k)
            merge_turns(sp, visit_load, lambda *a: None)
            gla(sp, visit_load, lambda *a: None)

            def y_loads(i, last):
                for k in range(Y_HALVES):
                    load_half(sp, phases["Y"], i, k)
                if isinstance(i, int) and i == 0:
                    for q in range(2):
                        sp.wait_ge(og_saved[q], 16 * (A_HEADS + 4 * B_HEADS) // 2)
                        sp.wait_ge(mg_saved[q], 16 * KT)
                    for q in range(8):
                        if q >= 2:
                            sp.wait_ge(o_lo_done, q - 1)
                        sp.dma_start(o_raw[q % 2][:, :, :],
                                     o_d[q // 4][4 * (q % 4):4 * (q % 4) + 4].rearrange("k p n -> p k n")
                                     ).then_inc(o_here[q % 2], 16)
                    sp.dma_start(mg_all[:, :, :, :], mg_d.rearrange("k p m n -> p k m n")).then_inc(m_here, 16)
            y_turns(sp, y_loads)

            def o_loads(i, last):
                for k in range(O_HALVES):
                    load_half(sp, phases["O"], i, k)
                    if isinstance(i, int) and k == 3 and i == 0:
                        sp.wait_ge(y_done, KT)
                        sp.wait_ge(half_used, phases["O"].n0)
                        sp.dma_start(gate_row[:, :], row_on_all(gate_d)).then_inc(rows_here, 16)
                        sp.dma_start(xres[:, :, :], x_v).then_inc(rows_here, 16)
                        sp.dma_start(fin_row[:, :], row_on_all(final_g)).then_inc(rows_here, 16)
            o_loads(0, False)
            with sp.Fori(1, phases["O"].turns) as i:
                o_loads(i, False)
            for tt in range(TT):
                sp.wait_ge(final_ready, tt + 1)
                sp.dma_start(out_v[:, tt, :], z[:, tt, :]).then_inc(out_saved, 16)
            sp.wait_ge(out_saved, 16 * TT)

        @block.gpsimd
        def _(pool):
            pool.wait_ge(gate_ready, 1)
            pool.dma_start(gate_d, ada_rows[0:1, 2 * D:3 * D]).then_inc(gate_saved, 16)
            pool.wait_ge(h_done, KT)
            pool.wait_ge(gate_saved, 16)
            pool.memset(gk_s[:, :, :], 0.0).then_inc(gk_zero, 1)
            pool.wait_ge(gk_zero, 1)

            def decay_weights(g):
                for s in range(2):
                    pool.dma_start(gk_s[s * RANK:(s + 1) * RANK, s, :],
                                   w_gk[0, s, :, bass.ds(g * B_DK, B_DK)]).then_inc(gk_here, 16)
            decay_weights(0)

            def save_a(p):
                pool.wait_ge(og_ready, p.n + 1)
                pool.dma_start(o_d[0][bass.ds(p.n, 1)].rearrange("k p n -> p (k n)"),
                               og[p.odd][:, :]).then_inc(og_saved[p.odd], 16)
            heads_of(pool, lambda own, p, last: None if p is None else save_a(p))

            def save_merge(m, i):
                pool.wait_ge(mg_ready, m * 2 + (i + 1))
                pool.dma_start(mg_d[bass.ds(m, 1), :, i, :].rearrange("k p n -> p (k n)"),
                               mg[i][:, :]).then_inc(mg_saved[i], 16)
            for i in range(2):
                save_merge(0, i)
            save_merge(1, 0)
            save_a(A_LAST)
            save_merge(1, 1)
            with pool.Fori(2, KT) as m:
                for i in range(2):
                    save_merge(m, i)

            def save_b(p):
                for j in range(4):
                    pool.wait_ge(og_ready, p * 4 + (OB + j + 1))
                    pool.dma_start(o_d[1][bass.ds(p * 4 + j, 1)].rearrange("k p n -> p (k n)"),
                                   og[j % 2][:, :]).then_inc(og_saved[j % 2], 16)
            pool.wait_ge(aux_in, aux_b(0, "z11") + 1)
            decay_weights(1)
            with pool.Fori(1, B_HEADS - 1) as g:
                save_b(g - 1)
                pool.wait_ge(aux_in, aux_b(g, "z11") + 1)
                decay_weights(g + 1)
            save_b(B_HEADS - 2)
            save_b(B_HEADS - 1)
            for q in range(2):
                pool.wait_ge(og_saved[q], 16 * (A_HEADS + 4 * B_HEADS) // 2)
                pool.wait_ge(mg_saved[q], 16 * KT)

        @block.scalar
        def _(act):
            act.wait_ge(c_here, 32)
            act.activation(c_sig[:, :, :], c_in[:, :, :], ACT.Sigmoid).then_inc(c_sig_done, 1)
            act.wait_ge(lb_a, 1)
            act.activation(lg[:, :, :], lg[:, :, :], ACT.Exp).then_inc(lb_b, 1)
            act.wait_ge(x_here, 32)
            act.wait_ge(memset_done, 1)
            for t in range(ALLT):
                if t:
                    act.drain()
                act.activation(sq0[:, :], xs[:, t, :], ACT.Square, accum_out=ssq0[:, t:t + 1])
            act.drain()
            act.activation(rstd0[:, :], ssq0[:, :], ACT.Ln, bias=eps_col[:, :], scale=1.0 / D)
            act.drain()
            act.activation(rstd0[:, :], rstd0[:, :], ACT.Exp, scale=-0.5).then_inc(rstd0_done, 1)

            def ada(i):
                for g in range(2):
                    act.wait_ge(ada_used, i * 16 + (8 * g + 8))
                    act.activation(ada_rows[:, bass.ds(i * 1024 + g * 512, 512)], ps_proj[g][0:2, :],
                                   ACT.Copy).then_inc(bank_read[g], 1)
            ada_pairs(act, ada)
            for kt in range(KT):
                act.wait_ge(h32_done, kt + 1)
                act.activation(h_hi[:, kt, :], h32[kt % 2][:, :], ACT.Copy).then_inc(h_hi_done, 1)

            for k in range(AHEAD):
                split_hi(act, (phases["A"], 0, k, False))

            def a_body(own, p, last):
                for t in range(A_SLOTS):
                    a_act(act, t, own, p)
                    if t % VISITS == 0:
                        split_hi(act, ahead("A", own.n, t // VISITS, own.odd, last))
            heads_of(act, a_body)

            def hi_ahead(name, turn, k, visit, tokens, last):
                if visit == 0:
                    split_hi(act, ahead(name, turn, k, False, last))

            def read_merge(m, i):
                unit_done(act, "M", m, i)
                if not known(m, 0):
                    act.wait_ge(mg_saved[i], m * 16)
                b = bank_of("M", i)
                act.activation(mg[i][:, :], ps_proj[b][:, 0:T], ACT.Sigmoid).then_inc(bank_read[b], 1)
                act.drain().then_inc(mg_ready, 1)

            def merge_steps(eng, name, turn, s, t):
                if name == "M" and s == 0:
                    if known(turn, 0):
                        unit_done(act, "R", 0, 0)
                        b = bank_of("R", 0)
                        act.activation(rT[:, :], ps_proj[b][0:2 * RANK, :], ACT.Copy).then_inc(bank_read[b], 1)
                        act.drain().then_inc(rT_ready, 1)
                    else:
                        read_merge(turn - 1, 1)
                if name == "M" and s == 4:
                    read_merge(turn, 0)
                if t is not None:
                    a_act(act, t, None, A_LAST)
            merge_turns(act, hi_ahead, merge_steps)
            read_merge(KT - 1, 1)
            gla(act, hi_ahead, b_act)

            for k in range(AHEAD):
                split_hi(act, (phases["Y"], 0, k, False))
            for q in range(8):
                act.wait_ge(o_here[q % 2], 16 * (q // 2 + 1))
                act.activation(o_hi[:, q // 4, 4 * (q % 4):4 * (q % 4) + 4, :], o_raw[q % 2][:, :, :],
                               ACT.Copy).then_inc(o_hi_done, 1)

            def y_hi_of(i):
                act.wait_ge(y32_ready, i + 1)
                act.activation(y_hi[:, bass.ds(i, 1), :].rearrange("p k n -> p (k n)"), y32[:, :],
                               ACT.Copy).then_inc(y_hi_done, 1)

            def y_body(i, last):
                for k in range(Y_HALVES):
                    if k == 1 and not known(i, 0):
                        y_hi_of(i - 1)
                    split_hi(act, ahead("Y", i, k, False, last))
            y_turns(act, y_body)
            y_hi_of(KT - 1)

            def o_body(i, last):
                for k in range(O_HALVES):
                    split_hi(act, ahead("O", i, k, False, last))
            with act.Fori(0, phases["O"].turns - 1) as i:
                o_body(i, False)
            o_body(phases["O"].turns - 1, True)
            act.wait_ge(z_ready, 2 * phases["O"].turns)
            for tt in range(TT):
                if tt:
                    act.drain()
                act.activation(zsq[:, :], z[:, tt, :], ACT.Square, accum_out=zss[:, tt:tt + 1])
            act.drain()
            act.activation(zr[:, :], zss[:, :], ACT.Ln, bias=eps_col[:, :], scale=1.0 / D)
            act.drain()
            act.activation(zr[:, :], zr[:, :], ACT.Exp, scale=-0.5).then_inc(zr_ready, 1)

        @block.tensor
        def _(pe):
            pe.wait_ge(consts_here, 16 * 10)
            pe.wait_ge(rows_ready, 1)
            for col, rows, n in ((0, lbr[:, 0, :], 32), (32, lbr[:, 1, :], 32), (64, rows16[:, 0, :], 16),
                                 (80, rows16[:, 1, :], 16), (96, rows16[:, 2, :], 16)):
                mm = pe.transpose(ps_turn[:, col:col + n], rows, ident[0:n, 0:n])
            mm.then_inc(cols_done, 1)
            pe.wait_ge(c_act_done, 1)

            def ada(i):
                for n in range(16):
                    g, q = divmod(n, 8)
                    if q == 0 and not known(i, 0):
                        pe.wait_ge(bank_read[g], i)
                    pe.wait_ge(raw_here[n % 4], i * 64 + 16 * (n // 4 + 1))
                    for jj in range(2):
                        kt = 2 * q + jj
                        mm = pe.matmul(ps_proj[g][0:2, :], c_act[:, kt, :], raw[n % 4][:, jj * 512:(jj + 1) * 512],
                                       start=kt == 0, stop=kt == KT - 1)
                    mm.then_inc(ada_used, 1)
            ada_pairs(pe, ada)
            for g in range(2):
                pe.wait_ge(bank_read[g], ADA_PAIRS)
            for s in range(2):
                for kt in range(KT):
                    mm = pe.transpose(ps_score[0][:, (s * KT + kt) * 2:(s * KT + kt) * 2 + 2],
                                      ada_rows[:, s * D + kt:(s + 1) * D:KT], ident[0:2, 0:2])
            mm.then_inc(adacol_done, 1)
            pe.wait_ge(xn_done, ALLT)
            for kt in range(KT):
                if kt >= 2:
                    pe.wait_ge(h32_done, kt - 1)
                for t in range(ALLT):
                    mm = pe.transpose(ps_o[kt % 2][:, t * P:(t + 1) * P], xs[:, t, kt::KT], ident[:, :])
                mm.then_inc(xT_done, 1)
            pe.wait_ge(h_done, KT)
            pe.wait_ge(gate_saved, 16)

            def a_body(own, p, last):
                for t in range(A_SLOTS):
                    k = t // VISITS
                    wide = (k // 2) in (1, 2, 3)
                    project(pe, "A", own.n, k, own.odd, own.pair, t % VISITS, NT if wide else T)
                    a_pe(pe, t, own, p)
            heads_of(pe, a_body)

            def unit_slot(name, turn, k, visit, tokens, last):
                project(pe, name, turn, k, 0, turn, visit, tokens)

            def merge_steps(eng, name, turn, s, t):
                if t is not None:
                    a_pe(pe, t, None, A_LAST)
            merge_turns(pe, unit_slot, merge_steps)
            gla(pe, unit_slot, b_pe)
            pe.wait_ge(o_lo_done, 8)

            def y_body(i, last):
                for k in range(Y_HALVES):
                    for visit in range(VISITS):
                        project(pe, "Y", i, k, 0, i, visit, T)
            y_turns(pe, y_body)
            pe.wait_ge(y_done, KT)

            def o_body(i):
                for k in range(O_HALVES):
                    slot = phases["O"].part_slot(False, k)
                    if k == 0:
                        for tt in range(TT):
                            bank_free(pe, "O", i, 0, tt)
                    pe.wait_ge(lo_done, phases["O"].number(i, k) + 1)
                    for jj in range(2):
                        kt = 2 * k + jj
                        hi, lo = w_hi[slot][:, jj * 512:(jj + 1) * 512], w_lo[slot][:, jj * 512:(jj + 1) * 512]
                        for tt in range(TT):
                            bank = ps_proj[bank_of("O", tt)]
                            y_h, y_l = y_hi[:, kt, tt * P:(tt + 1) * P], y_lo[:, kt, tt * P:(tt + 1) * P]
                            pe.matmul(bank[:, :], y_h, hi, start=kt == 0, stop=False)
                            pe.matmul(bank[:, :], y_h, lo, start=False, stop=False)
                            mm = pe.matmul(bank[:, :], y_l, hi, start=False, stop=kt == KT - 1)
                    mm.then_inc(half_used, 1)
            with pe.Fori(0, phases["O"].turns) as i:
                o_body(i)

        @block.vector
        def _(dve):
            dve.memset(ones[:, :], 1.0)
            dve.memset(one_col[:, :], 1.0)
            dve.memset(eps_col[:, :], EPS).then_inc(memset_done, 1)
            dve.wait_ge(c_sig_done, 1)
            dve.tensor_tensor(c_act[:, :, :].rearrange("p k c -> p c k"), c_in[:, :, :], c_sig[:, :, :],
                              ALU.mult).then_inc(c_act_done, 1)
            dve.wait_ge(consts_here, 16 * 10)
            dve.tensor_tensor(lmax[:, :], lg[:, 0, :], lg[:, 1, :], ALU.max)
            dve.drain()
            dve.tensor_tensor(lg[:, :, :], lg[:, :, :], strided(lmax[:, :], 0, [[0, 2], [1, P]]),
                              ALU.subtract).then_inc(lb_a, 1)
            dve.wait_ge(lb_b, 1)
            dve.tensor_tensor(lsum[:, :], lg[:, 0, :], lg[:, 1, :], ALU.add)
            dve.drain()
            dve.reciprocal(lsum[:, :], lsum[:, :])
            dve.drain()
            dve.tensor_tensor(lbr[:, 0, :], lg[:, 0, :], lsum[:, :], ALU.mult)
            dve.drain()
            dve.tensor_scalar(lbr[:, 1, :], lbr[:, 0, :], -1.0, 1.0, ALU.mult, ALU.add).then_inc(rows_ready, 1)
            dve.wait_ge(cols_done, 1)
            for col, dst, n in ((0, lb_cols, 32), (32, oml_cols, 32), (64, a_gain, 16), (80, b_gain, 16),
                                (96, bgk_cols, 16)):
                dve.tensor_copy(dst[:, :], ps_turn[:, col:col + n])
            dve.wait_ge(rstd0_done, 1)
            for t in range(ALLT):
                dve.tensor_scalar(xs[:, t, :], xs[:, t, :], rstd0[:, t:t + 1], None, ALU.mult).then_inc(xn_done, 1)
            dve.wait_ge(adacol_done, 1)
            cols = ps_score[0][:, 0:4 * KT].rearrange("p (s k c) -> p s k c", s=2, c=2)
            for src in range(2):
                dve.tensor_tensor(mod[:, src, :, :], cols[:, :, :, src], ada_b[:, :, :], ALU.add)
            dve.tensor_tensor(ada_rows[0:1, 2 * D:3 * D], ada_rows[0:1, 2 * D:3 * D], gate_b[:, :],
                              ALU.add).then_inc(gate_ready, 1)
            dve.drain()
            for src in range(2):
                dve.scalar_tensor_tensor(mod[:, src, 1, :], mod[:, src, 1, :], one_col[:, :], g_col[:, :],
                                         ALU.add, ALU.mult)
            dve.drain()

            def h_low(kt):
                dve.wait_ge(h_hi_done, kt + 1)
                dve.tensor_tensor(h_lo[:, kt, :], h32[kt % 2][:, :], h_hi[:, kt, :].bitcast(F32),
                                  ALU.subtract).then_inc(h_done, 1)
            for kt in range(KT):
                if kt >= 2:
                    dve.drain()
                dve.wait_ge(xT_done, kt + 1)
                for src in range(2):
                    mm = dve.tensor_scalar(h32[kt % 2][:, src * T:(src + 1) * T], ps_o[kt % 2][:, src * T:(src + 1) * T],
                                           mod[:, src, 1, kt:kt + 1], mod[:, src, 0, kt:kt + 1], ALU.mult, ALU.add)
                mm.then_inc(h32_done, 1)
                if kt:
                    h_low(kt - 1)
            h_low(KT - 1)

            for k in range(AHEAD):
                split_lo(dve, (phases["A"], 0, k, False))

            def a_body(own, p, last):
                for t in range(A_SLOTS):
                    if t % VISITS == 0:
                        split_lo(dve, ahead("A", own.n, t // VISITS, own.odd, last))
                    a_dve(dve, t, own, p)
            heads_of(dve, a_body)

            def lo_ahead(name, turn, k, visit, tokens, last):
                if visit == 0:
                    split_lo(dve, ahead(name, turn, k, False, last))

            def merge_steps(eng, name, turn, s, t):
                if t is not None:
                    a_dve(dve, t, None, A_LAST)
            merge_turns(dve, lo_ahead, merge_steps)
            gla(dve, lo_ahead, b_dve)

            for k in range(AHEAD):
                split_lo(dve, (phases["Y"], 0, k, False))
            for q in range(8):
                dve.wait_ge(o_hi_done, q + 1)
                part = (slice(None), q // 4, slice(4 * (q % 4), 4 * (q % 4) + 4), slice(None))
                dve.tensor_tensor(o_lo[part], o_raw[q % 2][:, :, :], o_hi[part].bitcast(F32),
                                  ALU.subtract).then_inc(o_lo_done, 1)
            dve.wait_ge(m_here, 16)

            def gates(i, m):
                return mg_all[:, bass.ds(i, 1), m, :].rearrange("p k n -> p (k n)")

            def y_sum(i):
                b = bank_of("Y", 1)
                dve.drain()
                unit_done(dve, "Y", i, 1)
                if not known(i, 0):
                    dve.wait_ge(y_hi_done, i)
                dve.tensor_tensor(y32[:, :], ps_proj[b][:, 0:T], gates(i, 1), ALU.mult).then_inc(bank_read[b], 1)
                dve.drain()
                dve.tensor_tensor(y32[:, :], y32[:, :], ya[:, :], ALU.add).then_inc(y32_ready, 1)

            def y_low(i):
                dve.wait_ge(y_hi_done, i + 1)
                at = bass.ds(i, 1)
                dve.tensor_tensor(y_lo[:, at, :].rearrange("p k n -> p (k n)"), y32[:, :],
                                  y_hi[:, at, :].rearrange("p k n -> p (k n)").bitcast(F32),
                                  ALU.subtract).then_inc(y_done, 1)

            def y_body(i, last):
                for k in range(Y_HALVES):
                    split_lo(dve, ahead("Y", i, k, False, last))
                    if k == 0 and not known(i, 0):
                        y_sum(i - 1)
                    if k == 1 and not known(i, 0):
                        y_low(i - 1)
                    if k == 2:
                        b = bank_of("Y", 0)
                        dve.drain()
                        unit_done(dve, "Y", i, 0)
                        dve.tensor_tensor(ya[:, :], ps_proj[b][:, 0:T], gates(i, 0), ALU.mult).then_inc(bank_read[b], 1)
            y_turns(dve, y_body)
            y_sum(KT - 1)
            y_low(KT - 1)

            def z_of(i):
                if known(i, 0):
                    dve.wait_ge(rows_here, 48)
                at = bass.ds(i * 512, 512)
                for tt in range(TT):
                    b = bank_of("O", tt)
                    dve.wait_ge(half_used, phases["O"].number(i, O_HALVES - 1) + 1)
                    dve.tensor_tensor(z[:, tt, at], ps_proj[b][:, :], gate_row[:, at], ALU.mult).then_inc(bank_read[b], 1)
                dve.drain()
                for tt in range(TT):
                    dve.tensor_tensor(z[:, tt, at], z[:, tt, at], xres[:, tt, at], ALU.add).then_inc(z_ready, 1)

            def o_body(i, last):
                for k in range(O_HALVES):
                    split_lo(dve, ahead("O", i, k, False, last))
                    if k == 0 and not known(i, 0):
                        z_of(i - 1)
            o_body(0, False)
            o_body(1, False)
            with dve.Fori(2, phases["O"].turns - 1) as i:
                o_body(i, False)
            o_body(phases["O"].turns - 1, True)
            z_of(phases["O"].turns - 1)
            dve.wait_ge(zr_ready, 1)
            for tt in range(TT):
                dve.scalar_tensor_tensor(z[:, tt, :], z[:, tt, :], zr[:, tt:tt + 1], fin_row[:, :], ALU.mult,
                                         ALU.mult).then_inc(final_ready, 1)


_INS = ["x", "c", "ctx", "c_ctx", "w_ada", "b_ada", "norm_g", "w_in", "hgrn_lb_logits", "gla_w_gk", "gla_b_gk",
        "hgrn_onorm_g", "gla_onorm_g", "w_pa", "w_pb", "w_out", "final_norm_g"]


def kernel(**inputs):
    import numpy as _np
    import concourse.bacc as _bacc
    from concourse import mybir as _mybir
    from concourse.bass_utils import run_bass_kernel_spmd as _run

    nc = _bacc.Bacc("TRN2", target_bir_lowering=False, num_devices=1)
    arrays, args = {}, []

    def add(name, a):
        arrays[name] = a
        args.append(nc.dram_tensor(name, a.shape, _mybir.dt.from_np(a.dtype), kind="ExternalInput").ap())

    for name in _INS:
        add(f"in_{name}_dram", _np.ascontiguousarray(inputs[name]))
    add("ident_dram", _np.eye(P, dtype=_np.float32))
    token = _np.arange(P)
    pair = token[:, None] ^ token[None, :]
    sizes = 1 << _np.arange(P.bit_length() - 1)
    add("masks_dram", _np.ascontiguousarray(_np.stack([(pair >= s) & (pair < 2 * s) for s in sizes], axis=1)
                                            .astype(_np.uint32)))
    shape = (1, 256, 2048)
    args.append(nc.dram_tensor("out_dram", shape, F32, kind="ExternalOutput").ap())
    bass_hgrn2_gla_block(nc, *args)
    r = _run(nc, [arrays], core_ids=[0])
    return r.results[0]["out_dram"]
```

```python
from contextlib import ExitStack

import concourse.bass as bass
from concourse import mybir

F32 = mybir.dt.float32
F32R = mybir.dt.float32r
U32 = mybir.dt.uint32
ALU = mybir.AluOpType
ACT = mybir.ActivationFunctionType
AX = mybir.AxisListType

P = 128
GRID_ROWS = 4
EPS = 1e-6
GATE_NORMALIZER = 16.0
RANK = 16
A_HEADS = 16
B_HEADS = 4
B_DK = 256
B_DV = 512
RING = 4
D_RING = 8
AHEAD = 2
VISITS = 2


def strided(ap, offset, dims):
    return bass.AP(tensor=ap.tensor, offset=ap.offset + offset, ap=[list(ap.ap[0])] + [list(d) for d in dims])


def to_columns(ap):
    return ap.rearrange("p (r c) -> p c r", r=GRID_ROWS)


class Phase:

    def __init__(self, name, n0, turns, sources, early):
        self.name, self.n0, self.turns, self.per, self.sources = name, n0, turns, len(sources), sources
        self.ring, self.early = (RING, early) if n0 else (D_RING, 0)
        assert (turns == 1 or self.per % self.ring == 0) and early % D_RING == 0

    def number(self, turn, k):
        return turn * self.per + (self.n0 + k)

    def slot(self, k):
        return (self.n0 + k) % RING

    def raw_slot(self, k):
        return (self.n0 + k) % self.ring

    def arrived(self, turn, k):
        early = self.early // D_RING
        return turn * (16 * self.per // self.ring) + 16 * ((self.n0 - self.early + k) // self.ring + early + 1)

    def before(self, turn, k):
        first = isinstance(turn, int) and self.early <= self.number(turn, k) < self.early + RING
        return self.number(turn, k) - ((D_RING if first else self.ring) - 1)


def bass_hgrn2_gla_block(nc, x, c, ctx, c_ctx, w_ada, b_ada, norm_g, w_in, lb_logits, w_gk, b_gk,
                         a_norm_g, b_norm_g, w_pa, w_pb, w_out, final_g, ident_c, masks_c, ada_sel_c, out):
    T = x.shape[1]
    TC = ctx.shape[1]
    D = x.shape[2]
    KT = D // P
    HK = KT // 2
    NT = T + TC
    TT = T // P
    CT = TC // P
    ALLT = TT + CT
    LEVELS = T.bit_length() - 1
    MASKED = LEVELS - 1
    NS = LEVELS + 1
    BW = B_HEADS * B_DK
    COL = {}
    at = 0
    for name, width in (("aq", D), ("ai", D), ("aff", D), ("afb", D), ("ag", D), ("bq", BW), ("bk", BW),
                        ("bv", D), ("rank", 2 * RANK), ("bg", D), ("ma", D), ("mb", D)):
        COL[name] = at
        at += width
    assert at == w_in.shape[2] and T == 256 and TC == 256 and KT == 16

    w_in_v = w_in.rearrange("l (p k) n -> p (l k) n", k=KT)
    COL_GATE = 2 * D
    w_ada_v = w_ada.rearrange("l (p k) n -> p (l k) n", k=KT)
    w_pa_v = w_pa.rearrange("l (k p) n -> p (l k) n", p=P)
    w_pb_v = w_pb.rearrange("l (k p) n -> p (l k) n", p=P)
    w_out_v = w_out.rearrange("l (k p) n -> p (l k) n", p=P)
    x_v = x.rearrange("b (t p) d -> p (b t) d", p=P)
    ctx_v = ctx.rearrange("b (t p) d -> p (b t) d", p=P)
    out_v = out.rearrange("b (t p) d -> p (b t) d", p=P)

    o_d = nc.dram_tensor("o_scratch", (2 * KT, P, T), F32, kind="Internal").ap()
    mg_d = nc.dram_tensor("merge_scratch", (KT, P, 2, T), F32, kind="Internal").ap()
    gate_d = nc.dram_tensor("gate_scratch", (2, D), F32, kind="Internal").ap()

    with ExitStack() as stack:
        def sb(name, shape, dt=F32, on=stack):
            return on.enter_context(nc.sbuf_tensor(name, shape, dt))

        def ps(name):
            return stack.enter_context(nc.psum_tensor(name, [P, 512], F32))

        def sem(name):
            return stack.enter_context(nc.semaphore(name))

        ps_proj = [ps("ps_proj0"), ps("ps_proj1")]
        ps_score = [ps("ps_score0"), ps("ps_score1")]
        ps_aux = ps("ps_aux")
        ps_turn = ps("ps_turn")
        ps_o = [ps("ps_o0"), ps("ps_o1")]

        ident = sb("ident", [P, P])
        ones = sb("ones", [P, TC])
        one_col = sb("one_col", [P, 1])
        wait_mark = sb("wait_mark", [P, 1])
        eps_col = sb("eps_col", [P, 1])
        masks = sb("masks", [P, MASKED, P], U32)
        lb_cols = sb("lb_cols", [P, 2 * A_HEADS])
        oml_cols = sb("oml_cols", [P, 2 * A_HEADS])
        a_gain = sb("a_gain", [P, KT])
        b_gain = sb("b_gain", [P, KT])
        bgk_cols = sb("bgk_cols", [P, 2 * 2 * B_HEADS])
        raw = [sb(f"raw{i}", [P, HK * P]) for i in range(RING)]
        w_hi = [sb(f"w_hi{i}", [P, HK * P], F32R) for i in range(RING)]
        w_lo = [sb(f"w_lo{i}", [P, HK * P], F32R) for i in range(RING)]
        c4 = sb("c4", [P, KT, 4], F32R)
        gate_st = [sb(f"gate_st{i}", [2, P]) for i in range(2)]
        mg = [sb(f"mg{i}", [P, T]) for i in range(2)]

        d_stack = ExitStack()
        raw_more = [sb(f"raw_more{i}", [P, HK * P], F32, d_stack) for i in range(D_RING - RING)]
        d_stack.close()
        raw_buffers = raw + raw_more
        h_stack = ExitStack()
        h_hi = sb("h_hi", [P, KT, NT], F32R, h_stack)
        h_lo = sb("h_lo", [P, KT, NT], F32R, h_stack)

        s0 = ExitStack()
        xs = sb("xs", [P, ALLT, D], F32, s0)
        xT = sb("xT", [P, KT, NT], F32, s0)
        c_in = sb("c_in", [P, 2, KT], F32, s0)
        c_sig = sb("c_sig", [P, 2, KT], F32, s0)
        c_act = sb("c_act", [P, KT, 2], F32, s0)
        ada_rows = sb("ada_rows", [5, 2 * D], F32, s0)
        ada_sel = sb("ada_sel", [5, 2], F32, s0)
        g_col = sb("g_col", [P, KT], F32, s0)
        mod = sb("mod", [P, 2, 2, KT], F32, s0)
        ssq0 = sb("ssq0", [P, ALLT], F32, s0)
        rstd0 = sb("rstd0", [P, ALLT], F32, s0)
        lg = sb("lg", [2 * A_HEADS, 2, P], F32, s0)
        lmax = sb("lmax", [2 * A_HEADS, P], F32, s0)
        lsum = sb("lsum", [2 * A_HEADS, P], F32, s0)
        lbr = sb("lbr", [2 * A_HEADS, 2, P], F32, s0)
        rows16 = sb("rows16", [16, 3, P], F32, s0)
        s0.close()

        ms = ExitStack()
        qT = [sb(f"qT{i}", [P, T], F32, ms) for i in range(2)]
        f = [sb(f"f{i}", [P, 2, NT], F32, ms) for i in range(2)]
        kk = [sb(f"kk{i}", [P, 2, NT], F32, ms) for i in range(2)]
        tail = sb("tail", [P, 2, T], F32, ms)
        QK = [sb(f"QK{i}", [P, 2, T], F32, ms) for i in range(2)]
        k_ctx = sb("k_ctx", [P, 2, TC], F32, ms)
        k_tok = [sb(f"k_tok{i}", [P, 2, CT, P], F32, ms) for i in range(2)]
        vT = sb("vT", [P, NT], F32, ms)
        v = sb("v", [P, ALLT, B_DV], F32, ms)
        S0 = sb("S0", [P, 4, B_DV], F32, ms)
        scores = [sb(f"scores{i}", [P, TT, T], F32, ms) for i in range(2)]
        q_end = [sb(f"q_end{i}", [P, 2, T], F32, ms) for i in range(2)]
        ksum = sb("ksum", [P, T], F32, ms)
        gsig = sb("gsig", [P, T], F32, ms)
        gT = sb("gT", [P, 4, T], F32, ms)
        osq = sb("osq", [P, 4, T], F32, ms)
        rstd = sb("rstd", [P, T], F32, ms)
        on = sb("on", [P, T], F32, ms)
        og = [sb(f"og{i}", [P, T], F32, ms) for i in range(2)]
        rT = sb("rT", [2 * RANK, NT], F32, ms)
        gk_s = sb("gk_s", [2 * RANK, 2, B_DK], F32, ms)
        zab = sb("zab", [P, NT], F32, ms)
        zmin = sb("zmin", [P, NT], F32, ms)
        ms.close()
        os_ = ExitStack()
        o_hi = sb("o_hi", [P, 2 * KT, T], F32R, os_)
        o_lo = sb("o_lo", [P, 2 * KT, T], F32R, os_)
        o_raw = [sb(f"o_raw{i}", [P, 4, T], F32, os_) for i in range(2)]
        os_.close()
        h_stack.close()

        y_hi = sb("y_hi", [P, KT, T], F32R)
        y_lo = sb("y_lo", [P, KT, T], F32R)
        m_in = [sb(f"m_in{i}", [P, T]) for i in range(2)]
        ya = sb("ya", [P, T])
        y32 = sb("y32", [P, T])
        gate3 = sb("gate3", [3, D])
        z = sb("z", [P, TT, D])
        xres = sb("xres", [P, TT, D])
        fin_row = sb("fin_row", [P, D])
        gate_row = sb("gate_row", [P, D])
        zsq = sb("zsq", [P, 512])
        zss = sb("zss", [P, TT, 4])
        zr = sb("zr", [P, TT])

        c_here = sem("c_here")
        consts_here = sem("consts_here")
        x_here = sem("x_here")
        raw_here = [sem(f"raw_here{i}") for i in range(D_RING)]
        c_hi_done = sem("c_hi_done")
        c4_done = sem("c4_done")
        c_sig_done = sem("c_sig_done")
        c_act_done = sem("c_act_done")
        memset_done = sem("memset_done")
        lb_a = sem("lb_a")
        lb_b = sem("lb_b")
        rows_ready = sem("rows_ready")
        cols_done = sem("cols_done")
        adacol_done = sem("adacol_done")
        gate_ready = sem("gate_ready")
        gate_saved = [sem("gate_saved0"), sem("gate_saved1")]
        rstd0_done = sem("rstd0_done")
        xn_done = sem("xn_done")
        xT_done = sem("xT_done")
        xT_read = sem("xT_read")
        h32_done = sem("h32_done")
        h_hi_done = sem("h_hi_done")
        h_done = sem("h_done")
        hi_done = sem("hi_done")
        lo_done = sem("lo_done")
        half_used = sem("half_used")
        bank_read = [sem("bank_read0"), sem("bank_read1")]
        q_ready = sem("q_ready")
        kb_ready = sem("kb_ready")
        fsig_ready = sem("fsig_ready")
        gsig_ready = sem("gsig_ready")
        gT_done = sem("gT_done")
        kctx_ready = sem("kctx_ready")
        vT_ready = sem("vT_ready")
        turn_in = sem("turn_in")
        turn_out = sem("turn_out")
        aux_in = sem("aux_in")
        aux_out = sem("aux_out")
        qk_ready = sem("qk_ready")
        tail_ready = sem("tail_ready")
        score_done = sem("score_done")
        score_read = sem("score_read")
        scores_ready = sem("scores_ready")
        q_end_ready = sem("q_end_ready")
        o_done = sem("o_done")
        o_read = sem("o_read")
        osq_ready = sem("osq_ready")
        rstd_ready = sem("rstd_ready")
        og_ready = sem("og_ready")
        og_saved = [sem("og_saved0"), sem("og_saved1")]
        sp_ready = sem("sp_ready")
        lf_ready = sem("lf_ready")
        rT_ready = sem("rT_ready")
        gk_here = sem("gk_here")
        gk_zero = sem("gk_zero")
        mg_ready = sem("mg_ready")
        mg_saved = [sem("mg_saved0"), sem("mg_saved1")]
        o_here = [sem("o_here0"), sem("o_here1")]
        o_hi_done = sem("o_hi_done")
        o_lo_done = sem("o_lo_done")
        m_here = [sem("m_here0"), sem("m_here1")]
        gate3_here = sem("gate3_here")
        gate_rows_done = sem("gate_rows_done")
        gate_row_ready = sem("gate_row_ready")
        y32_ready = sem("y32_ready")
        y_hi_done = sem("y_hi_done")
        y_done = sem("y_done")
        rows_here = sem("rows_here")
        z_bank_read = sem("z_bank_read")
        z_ready = sem("z_ready")
        zss_ready = sem("zss_ready")
        zr_ready = sem("zr_ready")
        zsum_ready = sem("zsum_ready")
        zg_ready = sem("zg_ready")
        final_ready = [sem("final_ready0"), sem("final_ready1")]
        cols_read = sem("cols_read")
        out_saved = sem("out_saved")

        def of_w_in(name, scale=1, shift=0, n=P):
            def load(hf, i):
                first = i * 2 * (P // 2) if COL[name] == 0 else i * P + COL[name]
                return w_in_v[:, hf * HK:(hf + 1) * HK, bass.ds(first, n)]
            return [(load, hf, scale, shift, n) for hf in range(2)]

        def of_view(view, col=0):
            def load(hf, i):
                return view[:, hf * HK:(hf + 1) * HK, bass.ds(i * P + col, P)]
            return [(load, hf, 1, 0, P) for hf in range(2)]

        def of_w_out(q):
            return (lambda hf, i: w_out_v[:, 2 * q:2 * q + 2, bass.ds(i * 512, 512)], q, 1, 0, 512)

        def of_w_ada(g, q):
            return [(lambda hf, i: w_ada_v[:, 2 * q:2 * q + 2, bass.ds(i * 1024 + g * 512, 512)], q, 1, 0, 512)]

        M_HEAD = 3
        G_B, G_B4 = 1, B_HEADS
        b_k, b_q = [[of_w_in(c, 2, d) for d in range(2)] for c in ("bk", "bq")]
        b_v = [of_w_in("bv", 4, j) for j in range(4)]
        b_g = [of_w_in("bg", 4, j - 4) for j in range(4)]
        phases = {}
        n0 = 0
        for name, turns, src in (
                ("D", 2 * D // 1024, [of_w_ada(g, q) for g in range(2) for q in range(KT // 2)]),
                ("A", A_HEADS, [of_w_in(c) for c in ("aff", "aq", "afb", "ag", "ai")] + [of_view(w_ada_v, COL_GATE)]),
                ("R", 1, [of_w_in("rank", 0, 0, 2 * RANK)]),
                ("M0", M_HEAD, [of_w_in("ma"), of_w_in("mb")]),
                ("B0", 1, [b_k[0], b_q[0], b_k[1], b_q[1]] + b_v),
                ("B", B_HEADS - 1, [b_k[0], b_q[0], b_k[1], b_q[1], b_g[0], b_g[1],
                                    b_v[0], b_g[2], b_v[1], b_g[3], b_v[2], b_v[3]]),
                ("B4", 1, b_g),
                ("M", KT - M_HEAD, [of_w_in("ma", 1, M_HEAD), of_w_in("mb", 1, M_HEAD)]),
                ("Y", KT, [of_view(w_pa_v), of_view(w_pb_v)]),
                ("O", D // 512, [[of_w_out(q)] for q in range(KT // 2)])):
            phases[name] = Phase(name, n0, turns, sum(src, []), phases["D"].turns * phases["D"].per if n0 else 0)
            n0 += turns * phases[name].per
        order = list(phases)

        def ahead(name, turn, k, last):
            ph = phases[name]
            k += AHEAD
            if k < ph.per:
                return ph, turn, k
            if not last:
                return ph, turn + 1, k - ph.per
            k -= ph.per
            for nxt in order[order.index(name) + 1:]:
                q, rest = divmod(k, phases[nxt].per)
                if q < phases[nxt].turns:
                    return phases[nxt], q, rest
                k -= phases[nxt].per * phases[nxt].turns
            return None

        def split_hi(act, where):
            if where is None:
                return
            ph, turn, k = where
            s, n = ph.slot(k), (2 if ph.name in "DO" else HK) * ph.sources[k][4]
            act.wait_ge(raw_here[ph.raw_slot(k)], ph.arrived(turn, k))
            if not known(ph.number(turn, k), RING - 1):
                act.wait_ge(half_used, ph.number(turn, k) - (RING - 1))
            act.activation(w_hi[s][:, 0:n], raw_buffers[ph.raw_slot(k)][:, 0:n], ACT.Copy).then_inc(hi_done, 1)

        def split_lo(dve, where):
            if where is None:
                return
            ph, turn, k = where
            s, n = ph.slot(k), (2 if ph.name in "DO" else HK) * ph.sources[k][4]
            dve.wait_ge(hi_done, ph.number(turn, k) + 1)
            dve.tensor_tensor(w_lo[s][:, 0:n], raw_buffers[ph.raw_slot(k)][:, 0:n], w_hi[s][:, 0:n].bitcast(F32),
                              ALU.subtract).then_inc(lo_done, 1)

        def load_half(sp, ph, turn, k):
            load, hf, scale, shift, cols = ph.sources[k]
            s = ph.raw_slot(k)
            rows = 2 if ph.name in "DO" else HK
            head = {"B": G_B, "B4": G_B4}.get(ph.name, 0)
            if not known(ph.before(turn, k), 0):
                sp.wait_ge(lo_done, ph.before(turn, k))
            sp.dma_start(raw_buffers[s][:, 0:rows * cols].rearrange("p (k n) -> p k n", k=rows),
                         load(hf, turn * scale + (head * scale + shift))).then_inc(raw_here[s], 16)

        units = {name: ph.per // 2 for name, ph in phases.items()}
        units["D"] = units["O"] = 2
        first_pass = {}
        m0 = 0
        for name, per in units.items():
            first_pass[name] = m0
            m0 += per * phases[name].turns
            assert per % 2 == 0 or phases[name].turns == 1

        def bank_of(name, u):
            return (first_pass[name] + u) % 2

        def bank_free(eng, name, turn, u):
            m = first_pass[name] + u
            eng.wait_ge(bank_read[m % 2], turn * (units[name] // 2) + m // 2)

        def unit_done(eng, name, turn, u):
            eng.wait_ge(half_used, phases[name].number(turn, 2 * u + 1) + 1)

        def unit_done_d(eng, turn, g):
            eng.wait_ge(half_used, phases["D"].number(turn, 8 * g + 7) + 1)

        def project(pe, name, turn, k, visit, tokens):
            ph = phases[name]
            u, hf = divmod(k, 2)
            bank = ps_proj[bank_of(name, u)]
            slot, cols = ph.slot(k), ph.sources[k][4]
            if visit == 0:
                if hf == 0:
                    bank_free(pe, name, turn, u)
                pe.wait_ge(lo_done, ph.number(turn, k) + 1)
            n = HK // VISITS
            for j in range(visit * n, visit * n + n):
                kt = hf * HK + j
                if name == "A" and known(turn, 0) and u == 0:
                    pe.wait_ge(h_done, kt + 1)
                hi = w_hi[slot][:, j * cols:(j + 1) * cols]
                lo = w_lo[slot][:, j * cols:(j + 1) * cols]
                first, last = kt == 0, kt == KT - 1
                if name == "A" and u == 5:
                    pe.matmul(bank[0:2, 0:cols], c4[:, kt, 0:2], hi, start=first, stop=False)
                    mm = pe.matmul(bank[0:2, 0:cols], c4[:, kt, 0:2], lo, start=False, stop=last)
                    continue
                if name == "Y":
                    if known(turn, 0) and j % 4 == 0:
                        pe.wait_ge(o_lo_done, (u * KT + kt) // 4 + 1)
                    r_hi, r_lo = o_hi[:, u * KT + kt, :], o_lo[:, u * KT + kt, :]
                else:
                    r_hi, r_lo = h_hi[:, kt, 0:tokens], h_lo[:, kt, 0:tokens]
                pe.matmul(bank[0:cols, 0:tokens], hi, r_hi, start=first, stop=False)
                pe.matmul(bank[0:cols, 0:tokens], hi, r_lo, start=False, stop=False)
                mm = pe.matmul(bank[0:cols, 0:tokens], lo, r_hi, start=False, stop=last)
            if visit == VISITS - 1:
                mm.then_inc(half_used, 1)

        AUX_B, TURN_B = 2 * A_HEADS, 2 * A_HEADS

        def aux_b(g, what):
            if isinstance(g, int) and g == 0:
                return AUX_B + {"z00": 0, "z01": 1, "z10": 2, "z11": 3}[what]
            order = ["z00", "z01", "s0", "s1", "s2", "s3", "ss", "z10", "z11"]
            if isinstance(g, int) and g == B_HEADS:
                order = ["s0", "s1", "s2", "s3", "ss"]
            return g * 9 + (AUX_B + 4 - 9 + order.index(what))

        def turn_k(vh_turn, branch, d=0):
            return vh_turn * 2 + 1 if branch == "A" else vh_turn * 6 + (TURN_B + 2 * d)

        def turn_v(turn, branch, j=0):
            return turn * 2 if branch == "A" else turn * 6 + (TURN_B + (1, 3, 4, 5)[j])

        def known(n, least):
            return isinstance(n, int) and n <= least

        def decay_b(dve, g, d, direction):
            col = g * 2 + (direction * 2 * B_HEADS + d)
            dve.drain()
            dve.wait_ge(sp_ready, g * 4 + (2 * d + direction + 1))
            dve.tensor_scalar(zmin[:, :], ps_aux[:, :], bgk_cols[:, bass.ds(col, 1)], 0.0,
                              ALU.add, ALU.min).then_inc(aux_out, 1)
            dve.drain()
            dve.tensor_tensor(f[d][:, 1 - direction, T:NT], zmin[:, T:NT], zab[:, T:NT], ALU.subtract)
            dve.tensor_tensor(f[d][:, 1 - direction, 0:T].rearrange("p (c r) -> p c r", r=GRID_ROWS),
                              to_columns(zmin[:, 0:T]), to_columns(zab[:, 0:T]),
                              ALU.subtract).then_inc(lf_ready, 1)

        def context_keys(dve, b, kd, waits):
            dve.drain()
            for what, count in waits:
                dve.wait_ge(what, count)
            dve.tensor_tensor_scan(k_ctx[:, 0, TC - 2::-1], f[b][:, 1, NT - 1:T:-1], ones[:, 0:TC - 1], 1.0,
                                   ALU.mult, ALU.mult)
            dve.tensor_tensor_scan(k_ctx[:, 1, 1:TC], f[b][:, 0, T:NT - 1], ones[:, 0:TC - 1], 1.0,
                                   ALU.mult, ALU.mult)
            dve.tensor_copy(strided(k_ctx[:, 0, :], TC - 1, [[1, 2]]),
                            strided(kk[b][:, 0, :], NT - 1, [[kd - (TC - 1), 2]]))
            dve.drain()
            dims = [[TC + 1, 2], [1, TC - 1]]
            dve.tensor_tensor(strided(k_ctx[:, 0, :], 0, dims), strided(k_ctx[:, 0, :], 0, dims),
                              strided(kk[b][:, 0, :], T, [[kd + 1, 2], [1, TC - 1]]), ALU.mult).then_inc(kctx_ready, 1)

        def level(dve, vh, b, kd, lv):
            s = 1 << lv
            n = T // (2 * s)
            base = vh * NS
            q0, f0, k0, t0 = qT[b][:, :], f[b][:, 0, :], kk[b][:, 0, :], tail[:, 0, :]
            if lv == 0:
                dve.drain()
                dve.wait_ge(q_ready, vh + 1)
                dve.wait_ge(tail_ready, vh + 1)
                if not known(vh, 0):
                    dve.wait_ge(score_done, base)
                dve.tensor_tensor(ksum[:, :], kk[b][:, 0, 0:T], strided(k0, kd, [[1, T]]),
                                  ALU.add).then_inc(qk_ready, 1)
            if lv >= 2:
                dve.wait_ge(score_done, base + lv)
            q_out, k_out = QK[lv % 2][:, 0, :], QK[lv % 2][:, 1, :]
            pairs = [[s, 2], [2 * s, n], [1, s]]
            dve.tensor_tensor(strided(q_out, 0, pairs), strided(q0, 0, pairs),
                              strided(f0, 0, [[NT + s, 2], [2 * s, n], [1, s]]), ALU.mult)
            k_dims = [[kd + s, 2], [2 * s, n], [1, s]]
            if lv == 0:
                dve.tensor_copy(strided(k_out, 0, pairs), strided(k0, 0, k_dims)).then_inc(qk_ready, 1)
            else:
                dve.tensor_tensor(strided(k_out, 0, pairs), strided(k0, 0, k_dims),
                                  strided(t0, 0, [[T + s, 2], [2 * s, n], [1, s]]), ALU.mult).then_inc(qk_ready, 1)
            dve.drain()
            if lv < LEVELS - 1:
                t_dims = [[T + s, 2], [2 * s, n], [1, s]]
                dve.tensor_tensor(strided(t0, 0, t_dims), strided(t0, 0, t_dims),
                                  strided(f0, NT + 2 * s - 1, [[-(NT + 2 * s - 1), 2], [2 * s, n], [0, s]]), ALU.mult)
                dve.drain()
            f_dims = [[NT + s, 2], [2 * s, n], [1, s]]
            dve.tensor_tensor(strided(f0, 0, f_dims), strided(f0, 0, f_dims),
                              strided(f0, s, [[NT - 1, 2], [2 * s, n], [0, s]]), ALU.mult)
            dve.drain()

        def take_scores(dve, vh, b, i, drained, free=None):
            if not drained:
                dve.drain()
            if i == 0 and free is not None:
                dve.wait_ge(*free)
            dve.wait_ge(score_done, vh * NS + (i + 1))
            src = ps_score[i % 2][:, 0:T]
            blocks = strided(scores[b][:, 0, :], 0, [[T + P, 2], [1, P]])
            if i == 0:
                dve.tensor_copy(blocks, src.rearrange("p (t n) -> p t n", t=2)).then_inc(score_read, 1)
            elif i <= MASKED:
                dve.memset(wait_mark[:, :], 0.0)
                m = masks[:, i - 1, :]
                dve.copy_predicated(blocks, strided(m, 0, [[0, 2], [1, P]]),
                                    src.rearrange("p (t n) -> p t n", t=2)).then_inc(score_read, 1)
            else:
                dve.tensor_copy(strided(scores[b][:, 0, :], P, [[1, T]]), src).then_inc(score_read, 1)

        def queries_end(dve, vh, b, free):
            if free is not None:
                dve.wait_ge(*free)
            dve.tensor_tensor(q_end[b][:, :, :], strided(qT[b][:, :], 0, [[0, 2], [1, T]]),
                              strided(f[b][:, 0, :], 0, [[NT, 2], [1, T]]), ALU.mult).then_inc(q_end_ready, 1)

        def gate_silu(dve, name, u, n, at):
            dve.drain()
            dve.wait_ge(gsig_ready, n + 1)
            b = bank_of(name, u)
            dve.tensor_tensor(gT[:, at, :], ps_proj[b][:, 0:T], gsig[:, :], ALU.mult).then_inc(bank_read[b], 1)
            dve.drain().then_inc(gT_done, 1)

        def gate_output(dve, src, at, gain, rs, n, nb, saved, permuted):
            dve.drain()
            dve.wait_ge(rstd_ready, rs)
            dve.tensor_tensor(on[:, :], src, rstd[:, :], ALU.mult).then_inc(o_read, 1)
            dve.drain()
            if saved is not None:
                dve.wait_ge(og_saved[nb], saved)
            o_in, g_in, o_out = on[:, :], gT[:, at, :], og[nb][:, :]
            if permuted:
                o_in = o_in.rearrange("p (c r) -> p r c", r=GRID_ROWS)
                g_in = g_in.rearrange("p (r c) -> p r c", r=GRID_ROWS)
                o_out = o_out.rearrange("p (r c) -> p r c", r=GRID_ROWS)
            dve.scalar_tensor_tensor(o_out, o_in, gain, g_in, ALU.mult, ALU.mult).then_inc(og_ready, 1)

        def logit_steps(act, g, d, direction):
            n = aux_b(g, f"z{d}{direction}")
            i = g * 4 + (2 * d + direction)
            col = g * 2 + (direction * 2 * B_HEADS + d)
            act.wait_ge(aux_in, n + 1)
            if not known(i, 0):
                act.wait_ge(lf_ready, i)
            act.activation(zab[:, :], ps_aux[:, :], ACT.Abs, bias=bgk_cols[:, bass.ds(col, 1)])
            act.drain()
            act.activation(zab[:, :], zab[:, :], ACT.Exp, scale=-1.0)
            act.drain()
            act.activation(zab[:, :], zab[:, :], ACT.Ln, bias=one_col[:, :]).then_inc(sp_ready, 1)

        def decay_exp(act, g, d, direction):
            act.wait_ge(lf_ready, g * 4 + (2 * d + direction + 1))
            fd = f[d][:, 1 - direction, :]
            act.activation(fd, fd, ACT.Exp, scale=1.0 / GATE_NORMALIZER).then_inc(fsig_ready, 1)

        def norm_scale(act, src, n, width, before):
            act.wait_ge(aux_in, n + 1)
            if before is not None:
                act.wait_ge(o_read, before)
            act.activation(rstd[:, :], src, ACT.Ln, bias=eps_col[:, :], scale=1.0 / width).then_inc(aux_out, 1)
            act.drain()
            act.activation(rstd[:, :], rstd[:, :], ACT.Exp, scale=-0.5).then_inc(rstd_ready, 1)

        def set_tail(act, vh):
            if not known(vh, 0):
                act.wait_ge(qk_ready, vh * NS)
            act.activation(tail[:, 0, :], ones[:, 0:T], ACT.Copy)
            act.activation(tail[:, 1, :], ones[:, 0:T], ACT.Copy).then_inc(tail_ready, 1)

        def read_turned(act, n, dst):
            act.wait_ge(turn_in, n + 1)
            act.activation(dst, ps_turn[:, :].rearrange("p (t n) -> p t n", t=4), ACT.Copy).then_inc(turn_out, 1)

        def turn_four(pe, n, tiles, ready):
            pe.wait_ge(*ready)
            if not known(n, 0):
                pe.wait_ge(turn_out, n)
            for t, tile in enumerate(tiles):
                mm = pe.transpose(ps_turn[:, t * P:(t + 1) * P], tile, ident[:, :])
            mm.then_inc(turn_in, 1)

        def score_product(pe, vh, b, i):
            pe.wait_ge(qk_ready, vh * NS + (i + 1))
            if i < 2:
                if not known(vh, 0):
                    pe.wait_ge(score_read, vh * NS)
            else:
                pe.wait_ge(score_read, vh * NS + (i - 1))
            dst = ps_score[i % 2][:, 0:T]
            if i == 0:
                q, k = qT[b][:, :], ksum[:, :]
            else:
                q, k = QK[(i - 1) % 2][:, 0, :], QK[(i - 1) % 2][:, 1, :]
            for t in range(TT):
                tq = t if i <= MASKED else 1 - t
                mm = pe.matmul(dst[:, t * P:(t + 1) * P], k[:, t * P:(t + 1) * P], q[:, tq * P:(tq + 1) * P],
                               start=True, stop=True)
            mm.then_inc(score_done, 1)

        A_LEVELS = [0, 1, 3, 4, 6, 8, 9, 11]
        B_LEVELS = [0, 1, 3, 4, 6, 7, 9, 10]
        assert len(A_LEVELS) == len(B_LEVELS) == LEVELS

        def scan_dve(dve, t, levels, vh, b, kd, free):
            if t in levels:
                level(dve, vh, b, kd, levels.index(t))
            if t == 3:
                take_scores(dve, vh, b, 0, True, free)
            if t - 3 in levels:
                lv = levels.index(t - 3)
                take_scores(dve, vh, b, lv + 1, lv > 0 and any(levels[lv - 1] + 3 < at <= t for at in levels))
            if t == levels[-1] + 1:
                queries_end(dve, vh, b, free)

        def scan_pe(pe, t, levels, vh, b):
            if t == 2:
                score_product(pe, vh, b, 0)
            if t - 2 in levels:
                score_product(pe, vh, b, levels.index(t - 2) + 1)

        class Head:

            def __init__(self, pair, odd):
                self.pair, self.odd = pair, odd
                self.n = pair * 2 + odd

        A_SLOTS = 2 * VISITS * units["A"]
        A_FIRST = [Head(0, 0), Head(0, 1), Head(1, 0)]
        A_LAST = Head(A_HEADS // 2 - 1, 1)
        FF, Q, FB, G, V, GATE = range(6)
        A_WIDE = (FF, FB, V)

        def heads_of(eng, body):
            body(A_FIRST[0], None, False)
            body(A_FIRST[1], A_FIRST[0], False)
            body(A_FIRST[2], A_FIRST[1], False)
            with eng.Fori(1, A_HEADS // 2 - 1) as j:
                body(Head(j, 1), Head(j, 0), False)
                body(Head(j + 1, 0), Head(j, 1), False)
            body(A_LAST, Head(A_HEADS // 2 - 1, 0), True)

        def a_dve(dve, t, own, p):
            if p is not None:
                free = None if known(p.n, 1) else (o_done, p.n - 1)
                scan_dve(dve, t, A_LEVELS, p.n, p.odd, NT, free)
                if t == 14:
                    dve.drain().then_inc(scores_ready, 1)
                if t == 19:
                    gate_output(dve, ps_o[0][:, 0:T], p.odd, a_gain[:, bass.ds(p.n, 1)], p.n + 1, p.n, p.odd,
                                None if known(p.pair, 0) else p.pair * 16, False)
            if own is not None:
                if t == 14:
                    context_keys(dve, own.odd, NT, [(fsig_ready, own.n * 2 + 2)]
                                 + ([] if known(own.n, 0) else [(turn_in, own.n * 2 - 1)]))
                if t == 17:
                    gate_silu(dve, "A", G, own.n, own.odd)

        def a_act(act, t, own, p):
            if p is not None:
                if t == 0:
                    unit_done(act, "A", p.n, GATE)
                    if not known(p.pair, 0):
                        act.wait_ge(gate_saved[p.odd], p.pair * 16)
                    b = bank_of("A", GATE)
                    act.activation(gate_st[p.odd][:, :], ps_proj[b][0:2, 0:P], ACT.Copy).then_inc(bank_read[b], 1)
                    act.drain().then_inc(gate_ready, 1)
                    if not known(p.n, 0):
                        act.wait_ge(o_done, p.n)
                    read_turned(act, p.n * 2 + 1, v[:, :, 0:P])
                if t == 2:
                    act.wait_ge(aux_in, p.n * 2 + 1)
                    act.activation(S0[:, 0:2, 0:P], ps_aux[:, 0:2 * P].rearrange("p (s n) -> p s n", s=2),
                                   ACT.Copy).then_inc(aux_out, 1)
                if t == 16:
                    act.wait_ge(o_done, p.n + 1)
                    if not known(p.n, 0):
                        act.wait_ge(aux_in, p.n * 2)
                    act.activation(osq[:, 0, :], ps_o[0][:, 0:T], ACT.Square).then_inc(osq_ready, 1)
                if t == 18:
                    norm_scale(act, ps_aux[:, 0:T], p.n * 2 + 1, P, None if known(p.n, 0) else p.n)
            if own is not None:
                if t in (4, 12):
                    unit, direction = (FF, 0) if t == 4 else (FB, 1)
                    unit_done(act, "A", own.n, unit)
                    b = bank_of("A", unit)
                    if not known(own.n, 1):
                        act.wait_ge(q_end_ready, own.n - 1)
                    fd = f[own.odd][:, 1 - direction, :]
                    act.activation(fd, ps_proj[b][:, :], ACT.Sigmoid).then_inc(bank_read[b], 1)
                    act.drain()
                    col = own.n + direction * A_HEADS
                    act.activation(fd, fd, ACT.Identity, bias=lb_cols[:, bass.ds(col, 1)],
                                   scale=oml_cols[:, bass.ds(col, 1)])
                    act.drain()
                    act.activation(kk[own.odd][:, direction, :], fd, ACT.Identity, bias=one_col[:, :], scale=-1.0)
                    act.drain().then_inc(fsig_ready, 1)
                if t == 14:
                    set_tail(act, own.n)
                if t == 8:
                    unit_done(act, "A", own.n, Q)
                    if not known(own.n, 1):
                        act.wait_ge(q_end_ready, own.n - 1)
                    b = bank_of("A", Q)
                    act.activation(qT[own.odd][:, :], ps_proj[b][:, 0:T], ACT.Copy).then_inc(bank_read[b], 1)
                    act.drain().then_inc(q_ready, 1)
                if t == 16:
                    unit_done(act, "A", own.n, G)
                    if not known(own.n, 0):
                        act.wait_ge(gT_done, own.n)
                    act.activation(gsig[:, :], ps_proj[bank_of("A", G)][:, 0:T], ACT.Sigmoid).then_inc(gsig_ready, 1)
                if t == 18:
                    read_turned(act, own.n * 2, k_tok[own.odd][:, :, :, :].rearrange("p s t n -> p (s t) n"))
                if t == 20:
                    unit_done(act, "A", own.n, V)
                    b = bank_of("A", V)
                    if not known(own.n, 0):
                        act.wait_ge(turn_in, own.n * 2)
                    act.activation(vT[:, :], ps_proj[b][:, :], ACT.Copy).then_inc(bank_read[b], 1)
                    act.drain().then_inc(vT_ready, 1)

        def a_pe(pe, t, own, p):
            if p is not None:
                if t == 1:
                    pe.wait_ge(turn_out, p.n * 2 + 2)
                    if not known(p.n, 0):
                        pe.wait_ge(aux_out, p.n * 2)
                    for s in range(2):
                        for ct in range(CT):
                            mm = pe.matmul(ps_aux[:, s * P:(s + 1) * P], k_tok[p.odd][:, 1 - s, ct, :],
                                           v[:, TT + ct, 0:P], start=ct == 0, stop=ct == CT - 1)
                    mm.then_inc(aux_in, 1)
                scan_pe(pe, t, A_LEVELS, p.n, p.odd)
                if t == 15:
                    pe.wait_ge(scores_ready, p.n + 1)
                    pe.wait_ge(q_end_ready, p.n + 1)
                    pe.wait_ge(aux_out, p.n * 2 + 1)
                    if not known(p.n, 0):
                        pe.wait_ge(o_read, p.n)
                    dst = ps_o[0][:, 0:T]
                    for jt in range(TT):
                        pe.matmul(dst, v[:, jt, 0:P], scores[p.odd][:, jt, :], start=jt == 0, stop=False)
                    for s in range(2):
                        mm = pe.matmul(dst, S0[:, s, 0:P], q_end[p.odd][:, s, :], start=False, stop=s == 1)
                    mm.then_inc(o_done, 1)
                if t == 17:
                    pe.wait_ge(osq_ready, p.n + 1)
                    pe.matmul(ps_aux[:, 0:T], ones[:, 0:P], osq[:, 0, :], start=True, stop=True).then_inc(aux_in, 1)
            if own is not None:
                if t == 17:
                    turn_four(pe, own.n * 2, [k_ctx[:, i // CT, (i % CT) * P:(i % CT + 1) * P] for i in range(4)],
                              (kctx_ready, own.n + 1))
                if t == 21:
                    turn_four(pe, own.n * 2 + 1, [vT[:, i * P:(i + 1) * P] for i in range(4)], (vT_ready, own.n + 1))

        VB, OB, RB = A_HEADS, A_HEADS, A_HEADS

        B_GATES = [(4, (0, 20), (0, 22)), (5, (1, 0), (1, 2)), (7, (1, 8), (1, 10)), (9, (1, 16), (1, 18))]
        B4_GATES = [(0, (0, 4), (0, 22)), (1, (0, 8), (0, 22)), (2, (0, 12), (0, 23)), (3, (0, 16), (0, 23))]

        def b_dve(dve, t, g, d, p):
            if d == 0 and p is not None:
                scan_dve(dve, t, B_LEVELS, p * 2 + (VB + 1), 1, 0, (o_done, p * 4 + OB))
                if t == 13:
                    dve.drain()
                    dve.tensor_tensor(scores[0][:, :, :], scores[0][:, :, :], scores[1][:, :, :],
                                      ALU.add).then_inc(scores_ready, 1)
            if p is not None:
                for j, (u, (gd, gt), out_at) in enumerate(B_GATES if g is not None else B4_GATES):
                    if (d, t) == (gd, gt + 1):
                        gate_silu(dve, "B" if g is not None else "B4", u, p * 4 + (OB + j), j)
                    if (d, t) == out_at:
                        gate_output(dve, ps_o[j % 2][:, (j // 2) * T:(j // 2) * T + T], j,
                                    b_gain[:, bass.ds(p * 4 + j, 1)], p + (RB + 1), p * 4 + (OB + j), j % 2,
                                    p * 32 + (16 * (OB // 2) + 16 * (j // 2)), True)
            if d == 1 and g is not None:
                scan_dve(dve, t, B_LEVELS, g * 2 + VB, 0, 0, (o_done, g * 4 + OB))
            if g is not None:
                if t in (1, 3):
                    decay_b(dve, g, d, t // 2)
                if t == 9:
                    before = turn_k(g, "B", 0) + (1 if d == 1 else 0 if known(g, 0) else -3)
                    waits = [(fsig_ready, g * 4 + (2 * A_HEADS + 2 * d + 2)),
                             (kb_ready, g * 2 + (d + 1)), (turn_in, before)]
                    context_keys(dve, d, 0, waits)

        def b_act(act, t, g, d, p):
            name = "B0" if isinstance(g, int) and g == 0 else "B"
            turn = 0 if name == "B0" else g - 1 if g is not None else None
            if g is not None:
                if d == 0 and t in (4, 12):
                    tile = t // 8
                    unit_done(act, name, turn, 2 * tile)
                    b = bank_of(name, 2 * tile)
                    act.wait_ge(q_end_ready, g * 2 + (VB + tile - 1))
                    act.activation(kk[tile][:, 0, 0:T].rearrange("p (c r) -> p c r", r=GRID_ROWS),
                                   to_columns(ps_proj[b][:, 0:T]), ACT.Copy)
                    act.activation(kk[tile][:, 0, T:NT], ps_proj[b][:, T:NT], ACT.Copy).then_inc(bank_read[b], 1)
                    act.drain().then_inc(kb_ready, 1)
                if d == 0 and t in (8, 16):
                    tile = t // 8 - 1
                    unit_done(act, name, turn, 2 * tile + 1)
                    b = bank_of(name, 2 * tile + 1)
                    act.activation(qT[tile][:, :].rearrange("p (c r) -> p c r", r=GRID_ROWS),
                                   to_columns(ps_proj[b][:, 0:T]), ACT.Copy,
                                   scale=float(B_DK) ** -0.5).then_inc(bank_read[b], 1)
                    act.drain().then_inc(q_ready, 1)
                if t == 13:
                    set_tail(act, g * 2 + (VB + d))
                if t in (1, 3):
                    logit_steps(act, g, d, t // 2)
                if t in (2, 4):
                    decay_exp(act, g, d, t // 2 - 1)
                if t == 12:
                    read_turned(act, turn_k(g, "B", d), k_tok[d][:, :, :, :].rearrange("p s t n -> p (s t) n"))
                if d == 1 and t in (4, 12, 20):
                    b_v_in(act, name, turn, g, (4, 12, 20).index(t))
                if d == 1 and t in (6, 14, 22):
                    b_v_out(act, g, (6, 14, 22).index(t))
            if d == 0 and p is not None:
                if t == 0:
                    before = "B0" if isinstance(p, int) and p == 0 else "B"
                    b_v_in(act, before, 0 if before == "B0" else p - 1, p, 3)
                if t == 2:
                    b_v_out(act, p, 3)
                if t in (5, 6, 7, 8):
                    act.wait_ge(aux_in, aux_b(g if g is not None else B_HEADS, f"s{t - 5}") + 1)
                    if t == 5:
                        act.wait_ge(o_done, p * 4 + OB)
                    act.activation(S0[:, t - 5, :], ps_aux[:, :], ACT.Copy).then_inc(aux_out, 1)
                if t in (16, 17, 18, 19):
                    j = t - 16
                    act.wait_ge(o_done, p * 4 + (OB + j + 1))
                    if j == 0:
                        act.wait_ge(rstd_ready, p + RB)
                    act.activation(osq[:, j, :], ps_o[j % 2][:, (j // 2) * T:(j // 2) * T + T],
                                   ACT.Square).then_inc(osq_ready, 1)
                if t == 21:
                    norm_scale(act, ps_aux[:, 0:T], aux_b(g if g is not None else B_HEADS, "ss"), B_DV, p * 4 + OB)
            if p is not None:
                for j, (u, at, _) in enumerate(B_GATES if g is not None else B4_GATES):
                    if (d, t) == at:
                        gates = "B" if g is not None else "B4"
                        unit_done(act, gates, turn if g is not None else 0, u)
                        act.wait_ge(gT_done, p * 4 + (OB + j))
                        act.activation(gsig[:, :], ps_proj[bank_of(gates, u)][:, 0:T],
                                       ACT.Sigmoid).then_inc(gsig_ready, 1)

        def b_v_in(act, name, turn, g, j):
            u = (4 + j) if name == "B0" else (6, 8, 10, 11)[j]
            unit_done(act, name, turn, u)
            b = bank_of(name, u)
            act.wait_ge(turn_in, turn_v(g, "B", j))
            act.activation(vT[:, 0:T].rearrange("p (c r) -> p c r", r=GRID_ROWS), to_columns(ps_proj[b][:, 0:T]),
                           ACT.Copy)
            act.activation(vT[:, T:NT], ps_proj[b][:, T:NT], ACT.Copy).then_inc(bank_read[b], 1)
            act.drain().then_inc(vT_ready, 1)

        def b_v_out(act, g, j):
            if j == 0:
                act.wait_ge(o_done, g * 4 + OB)
            read_turned(act, turn_v(g, "B", j), v[:, :, j * P:(j + 1) * P])

        def b_pe(pe, t, g, d, p):
            if g is not None and t in (0, 2):
                direction = t // 2
                if t == 0 and d == 0:
                    pe.wait_ge(gk_here, g * 32 + 32)
                    pe.wait_ge(rT_ready, 1)
                n = aux_b(g, f"z{d}{direction}")
                pe.wait_ge(aux_out, n)
                pe.matmul(ps_aux[:, :], gk_s[:, direction, d * P:(d + 1) * P], rT[:, :], start=True,
                          stop=True).then_inc(aux_in, 1)
            if d == 0 and p is not None:
                if t == 1:
                    turn_four(pe, turn_v(p, "B", 3), [vT[:, i * P:(i + 1) * P] for i in range(4)],
                              (vT_ready, p * 4 + (A_HEADS + 4)))
                if t in (4, 5, 6, 7):
                    s = t - 4
                    n = aux_b(g if g is not None else B_HEADS, f"s{s}")
                    if s == 0:
                        pe.wait_ge(turn_out, turn_v(p, "B", 3) + 1)
                    pe.wait_ge(aux_out, n)
                    for ct in range(CT):
                        mm = pe.matmul(ps_aux[:, :], k_tok[s // 2][:, 1 - s % 2, ct, :], v[:, TT + ct, :],
                                       start=ct == 0, stop=ct == CT - 1)
                    mm.then_inc(aux_in, 1)
                scan_pe(pe, t, B_LEVELS, p * 2 + (VB + 1), 1)
                if t in (15, 16, 17, 18):
                    j = t - 15
                    if j == 0:
                        pe.wait_ge(scores_ready, p + (RB + 1))
                        pe.wait_ge(q_end_ready, p * 2 + (VB + 2))
                        pe.wait_ge(aux_out, aux_b(g if g is not None else B_HEADS, "s3") + 1)
                        pe.wait_ge(o_read, p * 4 + OB)
                    dst = ps_o[j % 2][:, (j // 2) * T:(j // 2) * T + T]
                    if j >= 2:
                        pe.wait_ge(osq_ready, p * 4 + (OB + j - 1))
                    for jt in range(TT):
                        pe.matmul(dst, v[:, jt, j * P:(j + 1) * P], scores[0][:, jt, :], start=jt == 0, stop=False)
                    for s in range(4):
                        mm = pe.matmul(dst, S0[:, s, j * P:(j + 1) * P], q_end[s // 2][:, s % 2, :],
                                       start=False, stop=s == 3)
                    mm.then_inc(o_done, 1)
                if t == 20:
                    pe.wait_ge(osq_ready, p * 4 + (OB + 4))
                    for j in range(4):
                        mm = pe.matmul(ps_aux[:, 0:T], ones[:, 0:P], osq[:, j, :], start=j == 0, stop=j == 3)
                    mm.then_inc(aux_in, 1)
            if d == 1 and g is not None:
                scan_pe(pe, t, B_LEVELS, g * 2 + VB, 0)
                if t in (5, 13, 21):
                    j = (5, 13, 21).index(t)
                    turn_four(pe, turn_v(g, "B", j), [vT[:, i * P:(i + 1) * P] for i in range(4)],
                              (vT_ready, g * 4 + (A_HEADS + j + 1)))
            if g is not None and t == 11:
                turn_four(pe, turn_k(g, "B", d), [k_ctx[:, i // CT, (i % CT) * P:(i % CT + 1) * P] for i in range(4)],
                          (kctx_ready, g * 2 + (VB + d + 1)))

        B_WIDE = {"B0": (0, 2, 4, 5, 6, 7), "B": (0, 2, 6, 8, 10, 11)}

        def gla(eng, unit_slot, steps, merge):
            def turn(name, tn, g, p, last):
                k = 0
                for d in range(2):
                    for t in range(24):
                        if name == "B" or t // 4 in ((0, 1, 2, 3) if d == 0 else (0, 2, 4, 5)):
                            unit_slot(name, tn, k, t % VISITS, NT if k // 2 in B_WIDE[name] else T, last)
                            k += t % VISITS == VISITS - 1
                        steps(eng, t, g, d, p)
            turn("B0", 0, 0, None, True)
            with eng.Fori(1, B_HEADS - 1) as g:
                turn("B", g - 1, g, g - 1, False)
            turn("B", B_HEADS - 2, B_HEADS - 1, B_HEADS - 2, True)
            for t in range(24):
                if t < 16:
                    unit_slot("B4", 0, t // VISITS, t % VISITS, T, True)
                else:
                    unit_slot("M", 0, (t - 16) // VISITS, t % VISITS, T, False)
                    merge(0, t - 16)
                steps(eng, t, None, 0, B_HEADS - 1)

        def merge_head(eng, unit_slot, merge, steps):
            for t in range(4):
                unit_slot("R", 0, t // VISITS, t % VISITS, NT, True)
                steps(eng, t, None, A_LAST)
            for t in range(8 * M_HEAD):
                unit_slot("M0", t // 8, t % 8 // VISITS, t % VISITS, T, t // 8 == M_HEAD - 1)
                merge(t // 8, t % 8)
                if t + 4 < A_SLOTS:
                    steps(eng, t + 4, None, A_LAST)

        QUADS = 2 * KT // 4

        def merge_rest(eng, unit_slot, merge, split_outputs):
            def tile(turn, last, split):
                for s in range(8):
                    unit_slot("M", turn, s // VISITS, s % VISITS, T, last)
                    merge(turn, s)
                    if split is not None and s % 4 == 0:
                        split_outputs(split + s // 4)
            tile(1, False, None)
            for n in range(QUADS // 2):
                tile(2 + n, False, 2 * n)
            with eng.Fori(2 + QUADS // 2, KT - M_HEAD - 1) as i:
                tile(i, False, None)
            tile(KT - M_HEAD - 1, True, None)

        block = stack.enter_context(nc.Block())

        def row_on_all(ap):
            return bass.AP(tensor=ap.tensor, offset=ap.offset, ap=[[0, P], [1, D]])

        def y_turns(eng, body):
            body(0, False)
            with eng.Fori(1, KT - 1) as i:
                body(i, False)
            body(KT - 1, True)

        def o_turns(body):
            for i in range(phases["O"].turns):
                body(i, i == phases["O"].turns - 1)

        def o_bank(i, tt):
            return ps_score[tt] if i % 2 else ps_proj[bank_of("O", tt)]

        X_AT = [3, 5, 7, 9]
        assert len(X_AT) == ALLT
        XT_AT = 24
        D_TURNS, D_HALVES = phases["D"].turns, phases["D"].per
        Y_HALVES, O_HALVES = phases["Y"].per, phases["O"].per
        CONSTS = 10

        @block.sync
        def _(sp):
            for dst, src in ((c_in[:, 0, :], c.rearrange("b (p k) -> p (b k)", k=KT)),
                             (c_in[:, 1, :], c_ctx.rearrange("(p k) -> p k", k=KT))):
                sp.dma_start(dst, src).then_inc(c_here, 16)

            def d_loads(turn):
                for k in range(D_HALVES):
                    load_half(sp, phases["D"], turn, k)
                    if known(turn, 0) and k in X_AT:
                        t = X_AT.index(k)
                        sp.dma_start(xs[:, t, :], (x_v if t < TT else ctx_v)[:, t % TT, :]).then_inc(x_here, 16)
            d_loads(0)
            with sp.Fori(1, D_TURNS) as turn:
                d_loads(turn)

            def a_loads(own, p, last):
                for k in range(phases["A"].per):
                    load_half(sp, phases["A"], own.n, k)
            heads_of(sp, a_loads)

            def visit_load(name, turn, k, visit, tokens, last):
                if visit == 0:
                    load_half(sp, phases[name], turn, k)
            merge_head(sp, visit_load, lambda *a: None, lambda *a: None)
            gla(sp, visit_load, lambda *a: None, lambda *a: None)
            merge_rest(sp, visit_load, lambda *a: None, lambda *a: None)

            def y_loads(i, last):
                for k in range(Y_HALVES):
                    load_half(sp, phases["Y"], i, k)
                if known(i, 0):
                    sp.wait_ge(half_used, phases["Y"].n0)
                    for q in range(2):
                        sp.wait_ge(gate_saved[q], 16 * A_HEADS // 2)
                    sp.dma_start(gate3[0:2, :], gate_d).then_inc(gate3_here, 16)
                    sp.dma_start(gate3[2:3, :], b_ada[:, COL_GATE:COL_GATE + D]).then_inc(gate3_here, 16)
            y_turns(sp, y_loads)

            def o_loads(i, last):
                for k in range(O_HALVES):
                    load_half(sp, phases["O"], i, k)
                    if known(i, 0) and k == RING - 1:
                        sp.wait_ge(half_used, phases["O"].n0)
                        sp.dma_start(xres[:, :, :], x_v).then_inc(rows_here, 16)
                        sp.dma_start(fin_row[:, :], row_on_all(final_g)).then_inc(rows_here, 16)
            o_turns(o_loads)
            for n in range(4):
                sp.wait_ge(final_ready[n // 2], n % 2 + 1)
                sp.dma_start(out_v[:, n // 2, (n % 2) * (D // 2):(n % 2 + 1) * (D // 2)],
                             z[:, n // 2, (n % 2) * (D // 2):(n % 2 + 1) * (D // 2)]).then_inc(out_saved, 16)
            sp.wait_ge(out_saved, 16 * 4)

        @block.gpsimd
        def _(pool):
            logits = lb_logits.rearrange("r (q p) -> q r p", p=P)
            for dst, src in ((ident[:, :], ident_c), (masks[:, :, :], masks_c), (lg[:, :, :], logits),
                             (ada_rows[4:5, :], b_ada[:, 0:2 * D]), (ada_sel[:, :], ada_sel_c),
                             (g_col[:, :], norm_g.rearrange("l (p k) -> p (l k)", k=KT)),
                             (rows16[:, 0, :], a_norm_g.rearrange("l (q p) -> (l q) p", p=P)),
                             (rows16[:, 1, :], b_norm_g.rearrange("l (q p) -> (l q) p", p=P)),
                             (rows16[0:8, 2, :], b_gk[:, 0].rearrange("l (q p) -> (l q) p", p=P)),
                             (rows16[8:16, 2, :], b_gk[:, 1].rearrange("l (q p) -> (l q) p", p=P))):
                pool.dma_start(dst, src).then_inc(consts_here, 16)
            pool.wait_ge(h_done, KT)
            pool.wait_ge(cols_read, 1)
            pool.memset(gk_s[:, :, :], 0.0).then_inc(gk_zero, 1)
            pool.wait_ge(gk_zero, 1)

            def decay_weights(g):
                for s in range(2):
                    pool.dma_start(gk_s[s * RANK:(s + 1) * RANK, s, :],
                                   w_gk[0, s, :, bass.ds(g * B_DK, B_DK)]).then_inc(gk_here, 16)
            decay_weights(0)

            def save_a(own, p, last=None):
                if p is None:
                    return
                pool.wait_ge(gate_ready, p.n + 1)
                pool.dma_start(gate_d[:, bass.ds(p.n * P, P)], gate_st[p.odd][:, :]).then_inc(gate_saved[p.odd], 16)
                pool.wait_ge(og_ready, p.n + 1)
                pool.dma_start(o_d[bass.ds(p.n, 1)].rearrange("k p n -> p (k n)"),
                               og[p.odd][:, :]).then_inc(og_saved[p.odd], 16)
            heads_of(pool, save_a)

            def save_merge(m, i):
                pool.wait_ge(mg_ready, m * 2 + (i + 1))
                pool.dma_start(mg_d[bass.ds(m, 1), :, i, :].rearrange("k p n -> p (k n)"),
                               mg[i][:, :]).then_inc(mg_saved[i], 16)
            save_merge(0, 0)
            save_merge(0, 1)
            save_a(None, A_LAST)
            for m in range(1, M_HEAD):
                for i in range(2):
                    save_merge(m, i)

            def save_b(p):
                for j in range(4):
                    pool.wait_ge(og_ready, p * 4 + (OB + j + 1))
                    pool.dma_start(o_d[bass.ds(p * 4 + (KT + j), 1)].rearrange("k p n -> p (k n)"),
                                   og[j % 2][:, :]).then_inc(og_saved[j % 2], 16)

            def next_weights(g):
                pool.wait_ge(aux_in, aux_b(g, "z11") + 1)
                decay_weights(g + 1)
            next_weights(0)

            def of_turn(g, more):
                pool.wait_ge(og_ready, g * 4 + (OB - 4 + 1))
                pool.dma_start(o_d[bass.ds(g * 4 + (KT - 4), 1)].rearrange("k p n -> p (k n)"),
                               og[0][:, :]).then_inc(og_saved[0], 16)
                if more:
                    next_weights(g)
                for j in range(1, 4):
                    pool.wait_ge(og_ready, g * 4 + (OB - 4 + j + 1))
                    pool.dma_start(o_d[bass.ds(g * 4 + (KT - 4 + j), 1)].rearrange("k p n -> p (k n)"),
                                   og[j % 2][:, :]).then_inc(og_saved[j % 2], 16)
            with pool.Fori(1, B_HEADS - 1) as g:
                of_turn(g, True)
            of_turn(B_HEADS - 1, False)
            save_merge(M_HEAD, 0)
            save_b(B_HEADS - 1)
            save_merge(M_HEAD, 1)
            for i in range(2):
                save_merge(M_HEAD + 1, i)
            for q in range(2):
                pool.wait_ge(og_saved[q], 16 * (A_HEADS + 4 * B_HEADS) // 2)

            def load_quad(q):
                if q >= 2:
                    pool.wait_ge(o_lo_done, q - 1)
                pool.dma_start(o_raw[q % 2][:, :, :], o_d[4 * q:4 * q + 4].rearrange("k p n -> p k n")
                               ).then_inc(o_here[q % 2], 16)
            for q in range(2):
                load_quad(q)
            for q in range(2, QUADS):
                save_merge(M_HEAD + 1 + q // 2, q % 2)
                load_quad(q)
            with pool.Fori(M_HEAD + 1 + QUADS // 2, KT) as m:
                for i in range(2):
                    save_merge(m, i)
            pool.wait_ge(half_used, phases["Y"].n0)
            for i in range(2):
                pool.wait_ge(mg_saved[i], 16 * KT)

            def load_merge(m):
                for i in range(2):
                    pool.dma_start(m_in[i][:, :], mg_d[bass.ds(m, 1), :, i, :].rearrange("k p n -> p (k n)")
                                   ).then_inc(m_here[i], 16)
            load_merge(0)
            with pool.Fori(1, KT) as m:
                pool.wait_ge(y32_ready, m)
                load_merge(m)

        @block.scalar
        def _(act):
            act.wait_ge(c_here, 32)
            act.activation(c_sig[:, :, :], c_in[:, :, :], ACT.Sigmoid).then_inc(c_sig_done, 1)
            act.wait_ge(c_act_done, 1)
            act.activation(c4[:, :, :].rearrange("p k (c s) -> p k c s", s=2)[:, :, :, 0], c_act[:, :, :],
                           ACT.Copy).then_inc(c_hi_done, 1)

            def square_x(t):
                if t == 0:
                    act.wait_ge(x_here, 16 * ALLT)
                    act.wait_ge(memset_done, 1)
                act.drain()
                act.activation(h_lo[:, 0:D // NT, :], xs[:, t, :].rearrange("p (k n) -> p k n", n=NT), ACT.Square,
                               accum_out=ssq0[:, t:t + 1])

            def norm_x():
                act.drain()
                act.activation(rstd0[:, :], ssq0[:, :], ACT.Ln, bias=eps_col[:, :], scale=1.0 / D)
                act.drain()
                act.activation(rstd0[:, :], rstd0[:, :], ACT.Exp, scale=-0.5).then_inc(rstd0_done, 1)
                act.wait_ge(lb_a, 1)
                act.activation(lg[:, :, :], lg[:, :, :], ACT.Exp).then_inc(lb_b, 1)

            def read_ada(turn, g):
                unit_done_d(act, turn, g)
                act.activation(ada_rows[0:4, bass.ds(turn * 1024 + g * 512, 512)], ps_proj[bank_of("D", g)][0:4, :],
                               ACT.Copy).then_inc(bank_read[bank_of("D", g)], 1)
            for k in range(AHEAD):
                split_hi(act, (phases["D"], 0, k))
            for turn in range(D_TURNS):
                for k in range(D_HALVES):
                    if k == 0 and turn:
                        read_ada(turn - 1, 1)
                    if k == 8:
                        read_ada(turn, 0)
                    split_hi(act, ahead("D", turn, k, turn == D_TURNS - 1))
                    if turn == 0 and k >= D_HALVES // 2 and k % 2:
                        square_x((k - D_HALVES // 2) // 2)
                    if turn == 1 and k == 0:
                        norm_x()
                    kt = (turn * D_HALVES + k - XT_AT) // 2
                    if k % 2 and 0 <= kt < KT:
                        act.wait_ge(xT_done, kt + 1)
                        act.activation(xT[:, kt, :], ps_o[kt % 2][:, :], ACT.Copy).then_inc(xT_read, 1)
            read_ada(D_TURNS - 1, 1)
            for kt in range(KT):
                act.wait_ge(h32_done, kt + 1)
                act.activation(h_hi[:, kt, :], xT[:, kt, :], ACT.Copy).then_inc(h_hi_done, 1)

            act.wait_ge(cols_read, 1)

            def a_body(own, p, last):
                for t in range(A_SLOTS):
                    if t % VISITS == 0:
                        split_hi(act, ahead("A", own.n, t // VISITS, last))
                    a_act(act, t, own, p)
            heads_of(act, a_body)

            def hi_ahead(name, turn, k, visit, tokens, last):
                if visit == 0:
                    split_hi(act, ahead(name, turn, k, last))

            def read_merge(name, turn, i):
                m = turn + (0 if name == "M0" else M_HEAD)
                unit_done(act, name, turn, i)
                if not known(m, 0):
                    act.wait_ge(mg_saved[i], m * 16)
                b = bank_of(name, i)
                act.activation(mg[i][:, :], ps_proj[b][:, 0:T], ACT.Sigmoid).then_inc(bank_read[b], 1)
                act.drain().then_inc(mg_ready, 1)

            def merge_first(turn, s):
                if s == 0 and turn:
                    read_merge("M0", turn - 1, 1)
                if s == 4:
                    read_merge("M0", turn, 0)
                if s == 0 and turn == 0:
                    unit_done(act, "R", 0, 0)
                    b = bank_of("R", 0)
                    act.activation(rT[:, :], ps_proj[b][0:2 * RANK, :], ACT.Copy).then_inc(bank_read[b], 1)
                    act.drain().then_inc(rT_ready, 1)

            def merge(turn, s):
                if s == 0 and not known(turn, 0):
                    read_merge("M", turn - 1, 1)
                if s == 4:
                    read_merge("M", turn, 0)
            merge_head(act, hi_ahead, merge_first, a_act)
            read_merge("M0", M_HEAD - 1, 1)
            gla(act, hi_ahead, b_act, merge)

            def split_outputs(q):
                act.wait_ge(o_here[q % 2], 16 * (q // 2 + 1))
                act.activation(o_hi[:, 4 * q:4 * q + 4, :], o_raw[q % 2][:, :, :], ACT.Copy).then_inc(o_hi_done, 1)
            merge_rest(act, hi_ahead, merge, split_outputs)
            read_merge("M", KT - M_HEAD - 1, 1)

            def y_hi_of(i):
                act.wait_ge(y32_ready, i + 1)
                act.activation(y_hi[:, bass.ds(i, 1), :].rearrange("p k n -> p (k n)"), y32[:, :],
                               ACT.Copy).then_inc(y_hi_done, 1)

            def y_body(i, last):
                for k in range(Y_HALVES):
                    if k == 1 and not known(i, 0):
                        y_hi_of(i - 1)
                    split_hi(act, ahead("Y", i, k, last))
            y_turns(act, y_body)
            y_hi_of(KT - 1)
            act.wait_ge(gate_rows_done, 1)
            act.wait_ge(half_used, phases["O"].n0)
            for n, bank in enumerate((ps_o[0], ps_o[1], ps_turn, ps_aux)):
                mm = act.activation(gate_row[:, n * 512:(n + 1) * 512], bank[:, :], ACT.Copy)
            mm.then_inc(gate_row_ready, 1)

            def squares(i):
                for tt in range(TT):
                    act.drain()
                    act.wait_ge(z_ready, i * TT + (tt + 1))
                    act.activation(zsq[:, :], z[:, tt, bass.ds(i * 512, 512)], ACT.Square,
                                   accum_out=zss[:, tt, bass.ds(i, 1)])

            def o_body(i, last):
                for k in range(O_HALVES):
                    split_hi(act, ahead("O", i, k, last))
                    if k == 2 and not known(i, 0):
                        squares(i - 1)
            o_turns(o_body)
            act.preload_act_table(ACT.Ln)
            squares(phases["O"].turns - 1)
            act.drain().then_inc(zss_ready, 1)
            act.wait_ge(zsum_ready, 1)
            act.activation(zr[:, :], zr[:, :], ACT.Ln, bias=eps_col[:, :], scale=1.0 / D)
            act.drain()
            act.activation(zr[:, :], zr[:, :], ACT.Exp, scale=-0.5).then_inc(zr_ready, 1)
            act.drain()
            act.wait_ge(zg_ready, 2)
            for hf in range(2):
                part = z[:, 1, hf * (D // 2):(hf + 1) * (D // 2)]
                act.activation(part, part, ACT.Copy, scale=zr[:, 1:2]).then_inc(final_ready[1], 1)

        @block.tensor
        def _(pe):
            pe.wait_ge(c4_done, 1)

            def d_half(turn, k):
                ph = phases["D"]
                g, q = divmod(k, 8)
                bank = ps_proj[bank_of("D", g)]
                if q == 0 and turn:
                    bank_free(pe, "D", turn, g)
                pe.wait_ge(lo_done, ph.number(turn, k) + 1)
                s = ph.slot(k)
                for jj in range(2):
                    kt = 2 * q + jj
                    pe.matmul(bank[0:4, :], c4[:, kt, :], w_hi[s][:, jj * 512:(jj + 1) * 512], start=kt == 0,
                              stop=False)
                    mm = pe.matmul(bank[0:4, :], c4[:, kt, :], w_lo[s][:, jj * 512:(jj + 1) * 512], start=False,
                                   stop=kt == KT - 1)
                mm.then_inc(half_used, 1)

            def ada_column(s, kt):
                return pe.matmul(ps_score[0][:, (s * KT + kt) * 2:(s * KT + kt) * 2 + 2],
                                 ada_rows[:, s * D + kt:(s + 1) * D:KT], ada_sel[:, :], start=True, stop=True)

            for turn in range(D_TURNS):
                for k in range(D_HALVES):
                    d_half(turn, k)
                    if turn == D_TURNS - 1:
                        if k == 0:
                            for g in range(2):
                                pe.wait_ge(bank_read[g], D_TURNS // 2)
                        ada_column(0, k)
                    if turn == 1 and k == 11:
                        pe.wait_ge(consts_here, 16 * CONSTS)
                        pe.wait_ge(rows_ready, 1)
                        for col, rows, n in ((0, lbr[:, 0, :], 32), (32, lbr[:, 1, :], 32), (64, rows16[:, 0, :], 16),
                                             (80, rows16[:, 1, :], 16), (96, rows16[:, 2, :], 16)):
                            mm = pe.transpose(ps_turn[:, col:col + n], rows, ident[0:n, 0:n])
                        mm.then_inc(cols_done, 1)
                    kt = (turn * D_HALVES + k - XT_AT) // 2
                    if k % 2 == 0 and 0 <= kt < KT:
                        if kt == 0:
                            pe.wait_ge(xn_done, ALLT)
                        if kt >= 2:
                            pe.wait_ge(xT_read, kt - 1)
                        for t in range(ALLT):
                            mm = pe.transpose(ps_o[kt % 2][:, t * P:(t + 1) * P], xs[:, t, kt::KT], ident[:, :])
                        mm.then_inc(xT_done, 1)
            for g in range(2):
                pe.wait_ge(bank_read[g], D_TURNS)
            for kt in range(KT):
                mm = ada_column(1, kt)
            mm.then_inc(adacol_done, 1)

            def a_body(own, p, last):
                for t in range(A_SLOTS):
                    k = t // VISITS
                    project(pe, "A", own.n, k, t % VISITS, NT if k // 2 in A_WIDE else T)
                    a_pe(pe, t, own, p)
            heads_of(pe, a_body)

            def unit_slot(name, turn, k, visit, tokens, last):
                project(pe, name, turn, k, visit, tokens)
            merge_head(pe, unit_slot, lambda *a: None, a_pe)
            gla(pe, unit_slot, b_pe, lambda *a: None)
            merge_rest(pe, unit_slot, lambda *a: None, lambda *a: None)

            def y_body(i, last):
                for k in range(Y_HALVES):
                    for visit in range(VISITS):
                        project(pe, "Y", i, k, visit, T)
            y_turns(pe, y_body)
            pe.wait_ge(gate3_here, 32)
            for n, bank in enumerate((ps_o[0], ps_o[1], ps_turn, ps_aux)):
                mm = pe.matmul(bank[:, :], ones[0:3, 0:P], gate3[:, n * 512:(n + 1) * 512], start=True, stop=True)
            mm.then_inc(gate_rows_done, 1)

            def o_body(i, last):
                for k in range(O_HALVES):
                    slot = phases["O"].slot(k)
                    if k == 0:
                        for tt in range(TT):
                            if i == 0:
                                bank_free(pe, "O", i, tt)
                            elif i == 1:
                                pe.wait_ge(score_read, 2 * (A_HEADS // 2 + B_HEADS) * NS)
                            else:
                                pe.wait_ge(z_bank_read, (i - 2) * TT + tt + 1)
                    pe.wait_ge(lo_done, phases["O"].number(i, k) + 1)
                    if k == KT // 2 - 1 and known(i, 0):
                        pe.wait_ge(y_done, KT)
                    for jj in range(2):
                        kt = 2 * k + jj
                        hi, lo = w_hi[slot][:, jj * 512:(jj + 1) * 512], w_lo[slot][:, jj * 512:(jj + 1) * 512]
                        for tt in range(TT):
                            bank = o_bank(i, tt)
                            y_h, y_l = y_hi[:, kt, tt * P:(tt + 1) * P], y_lo[:, kt, tt * P:(tt + 1) * P]
                            pe.matmul(bank[:, :], y_h, hi, start=kt == 0, stop=False)
                            pe.matmul(bank[:, :], y_h, lo, start=False, stop=False)
                            mm = pe.matmul(bank[:, :], y_l, hi, start=False, stop=kt == KT - 1)
                    mm.then_inc(half_used, 1)
            pe.wait_ge(y_done, KT - 1)
            o_turns(o_body)

        @block.vector
        def _(dve):
            dve.memset(ones[:, :], 1.0)
            dve.memset(one_col[:, :], 1.0)
            dve.memset(eps_col[:, :], EPS).then_inc(memset_done, 1)
            dve.wait_ge(c_sig_done, 1)
            dve.tensor_tensor(c_act[:, :, :].rearrange("p k c -> p c k"), c_in[:, :, :], c_sig[:, :, :],
                              ALU.mult).then_inc(c_act_done, 1)
            dve.wait_ge(c_hi_done, 1)
            parts = c4[:, :, :].rearrange("p k (c s) -> p k c s", s=2)
            dve.tensor_tensor(parts[:, :, :, 1], c_act[:, :, :], parts[:, :, :, 0].bitcast(F32),
                              ALU.subtract).then_inc(c4_done, 1)

            def bounds():
                dve.wait_ge(consts_here, 16 * CONSTS)
                dve.tensor_tensor(lmax[:, :], lg[:, 0, :], lg[:, 1, :], ALU.max)
                dve.drain()
                dve.tensor_tensor(lg[:, :, :], lg[:, :, :], strided(lmax[:, :], 0, [[0, 2], [1, P]]),
                                  ALU.subtract).then_inc(lb_a, 1)

            def bounds_end():
                dve.wait_ge(lb_b, 1)
                dve.tensor_tensor(lsum[:, :], lg[:, 0, :], lg[:, 1, :], ALU.add)
                dve.drain()
                dve.reciprocal(lsum[:, :], lsum[:, :])
                dve.drain()
                dve.tensor_tensor(lbr[:, 0, :], lg[:, 0, :], lsum[:, :], ALU.mult)
                dve.drain()
                dve.tensor_scalar(lbr[:, 1, :], lbr[:, 0, :], -1.0, 1.0, ALU.mult, ALU.add).then_inc(rows_ready, 1)

            for k in range(AHEAD):
                split_lo(dve, (phases["D"], 0, k))
            for turn in range(D_TURNS):
                for k in range(D_HALVES):
                    split_lo(dve, ahead("D", turn, k, turn == D_TURNS - 1))
                    if turn == 0 and k == 8:
                        bounds()
                    if turn == 1 and k < 2 * ALLT and k % 2 == 0:
                        t = k // 2
                        if t == 0:
                            dve.wait_ge(rstd0_done, 1)
                        dve.tensor_scalar(xs[:, t, :], xs[:, t, :], rstd0[:, t:t + 1], None,
                                          ALU.mult).then_inc(xn_done, 1)
                    if turn == 1 and k == 7:
                        bounds_end()
                    if turn == 1 and k == 14:
                        dve.wait_ge(cols_done, 1)
                        for col, dst, n in ((0, lb_cols, 32), (32, oml_cols, 32), (64, a_gain, 16), (80, b_gain, 16),
                                            (96, bgk_cols, 16)):
                            mm = dve.tensor_copy(dst[:, :], ps_turn[:, col:col + n])
                        mm.then_inc(cols_read, 1)
            dve.wait_ge(adacol_done, 1)
            cols = ps_score[0][:, 0:4 * KT].rearrange("p (s k c) -> p s k c", s=2, c=2)
            for src in range(2):
                dve.tensor_copy(mod[:, src, 0, :], cols[:, 0, :, src])
                dve.scalar_tensor_tensor(mod[:, src, 1, :], cols[:, 1, :, src], one_col[:, :], g_col[:, :],
                                         ALU.add, ALU.mult)
            dve.drain()

            def h_low(kt):
                dve.wait_ge(h_hi_done, kt + 1)
                dve.tensor_tensor(h_lo[:, kt, :], xT[:, kt, :], h_hi[:, kt, :].bitcast(F32),
                                  ALU.subtract).then_inc(h_done, 1)
            for kt in range(KT):
                if kt == 0:
                    dve.wait_ge(xT_read, KT)
                for src in range(2):
                    part = xT[:, kt, src * T:(src + 1) * T]
                    mm = dve.tensor_scalar(part, part, mod[:, src, 1, kt:kt + 1], mod[:, src, 0, kt:kt + 1],
                                           ALU.mult, ALU.add)
                mm.then_inc(h32_done, 1)
                if kt:
                    h_low(kt - 1)
            h_low(KT - 1)

            def a_body(own, p, last):
                for t in range(A_SLOTS):
                    if t % VISITS == 0:
                        split_lo(dve, ahead("A", own.n, t // VISITS, last))
                    a_dve(dve, t, own, p)
            heads_of(dve, a_body)

            def lo_ahead(name, turn, k, visit, tokens, last):
                if visit == 0:
                    split_lo(dve, ahead(name, turn, k, last))

            def split_outputs(q):
                dve.wait_ge(o_hi_done, q + 1)
                dve.tensor_tensor(o_lo[:, 4 * q:4 * q + 4, :], o_raw[q % 2][:, :, :],
                                  o_hi[:, 4 * q:4 * q + 4, :].bitcast(F32), ALU.subtract).then_inc(o_lo_done, 1)
            merge_head(dve, lo_ahead, lambda *a: None, a_dve)
            gla(dve, lo_ahead, b_dve, lambda *a: None)
            merge_rest(dve, lo_ahead, lambda *a: None, split_outputs)

            def y_sum(i):
                b = bank_of("Y", 1)
                dve.drain()
                unit_done(dve, "Y", i, 1)
                dve.wait_ge(m_here[1], i * 16 + 16)
                if not known(i, 0):
                    dve.wait_ge(y_hi_done, i)
                dve.tensor_tensor(y32[:, :], ps_proj[b][:, 0:T], m_in[1][:, :], ALU.mult).then_inc(bank_read[b], 1)
                dve.drain()
                dve.tensor_tensor(y32[:, :], y32[:, :], ya[:, :], ALU.add).then_inc(y32_ready, 1)

            def y_low(i):
                dve.wait_ge(y_hi_done, i + 1)
                at = bass.ds(i, 1)
                dve.tensor_tensor(y_lo[:, at, :].rearrange("p k n -> p (k n)"), y32[:, :],
                                  y_hi[:, at, :].rearrange("p k n -> p (k n)").bitcast(F32),
                                  ALU.subtract).then_inc(y_done, 1)

            def y_body(i, last):
                for k in range(Y_HALVES):
                    split_lo(dve, ahead("Y", i, k, last))
                    if k == 0 and not known(i, 0):
                        y_sum(i - 1)
                    if k == 1 and not known(i, 0):
                        y_low(i - 1)
                    if k == 2:
                        b = bank_of("Y", 0)
                        dve.drain()
                        unit_done(dve, "Y", i, 0)
                        dve.wait_ge(m_here[0], i * 16 + 16)
                        dve.tensor_tensor(ya[:, :], ps_proj[b][:, 0:T], m_in[0][:, :],
                                          ALU.mult).then_inc(bank_read[b], 1)
            y_turns(dve, y_body)
            y_sum(KT - 1)
            y_low(KT - 1)

            def z_of(i, part):
                at = slice(i * 512, (i + 1) * 512)
                if part == 0:
                    if i == 0:
                        dve.wait_ge(gate_row_ready, 1)
                    dve.wait_ge(half_used, phases["O"].number(i, O_HALVES - 1) + 1)
                    for tt in range(TT):
                        dve.tensor_tensor(z[:, tt, at], o_bank(i, tt)[:, :], gate_row[:, at],
                                          ALU.mult).then_inc(z_bank_read, 1)
                else:
                    if i == 0:
                        dve.wait_ge(rows_here, 32)
                    dve.drain()
                    for tt in range(TT):
                        dve.tensor_tensor(z[:, tt, at], z[:, tt, at], xres[:, tt, at], ALU.add).then_inc(z_ready, 1)

            def o_body(i, last):
                for k in range(O_HALVES):
                    split_lo(dve, ahead("O", i, k, last))
                    if k < 2 and i:
                        z_of(i - 1, k)
            o_turns(o_body)
            for part in range(2):
                z_of(phases["O"].turns - 1, part)
            dve.wait_ge(zss_ready, 1)
            dve.tensor_reduce(zr[:, :], zss[:, :, :], AX.X, ALU.add).then_inc(zsum_ready, 1)
            for tt in (1, 0):
                for hf in range(2):
                    at = slice(hf * (D // 2), (hf + 1) * (D // 2))
                    if tt == 1:
                        dve.tensor_tensor(z[:, 1, at], z[:, 1, at], fin_row[:, at], ALU.mult).then_inc(zg_ready, 1)
                    else:
                        if hf == 0:
                            dve.wait_ge(zr_ready, 1)
                        dve.scalar_tensor_tensor(z[:, 0, at], z[:, 0, at], zr[:, 0:1], fin_row[:, at], ALU.mult,
                                                 ALU.mult).then_inc(final_ready[0], 1)


_INS = ["x", "c", "ctx", "c_ctx", "w_ada", "b_ada", "norm_g", "w_in", "hgrn_lb_logits", "gla_w_gk", "gla_b_gk",
        "hgrn_onorm_g", "gla_onorm_g", "w_pa", "w_pb", "w_out", "final_norm_g"]


def kernel(**inputs):
    import numpy as _np
    import concourse.bacc as _bacc
    from concourse import mybir as _mybir
    from concourse.bass_utils import run_bass_kernel_spmd as _run

    nc = _bacc.Bacc("TRN2", target_bir_lowering=False, num_devices=1)
    arrays, args = {}, []

    def add(name, a):
        arrays[name] = a
        args.append(nc.dram_tensor(name, a.shape, _mybir.dt.from_np(a.dtype), kind="ExternalInput").ap())

    for name in _INS:
        add(f"in_{name}_dram", _np.ascontiguousarray(inputs[name]))
    add("ident_dram", _np.eye(P, dtype=_np.float32))
    token = _np.arange(P)
    pair = token[:, None] ^ token[None, :]
    sizes = 1 << _np.arange(P.bit_length() - 1)
    add("masks_dram", _np.ascontiguousarray(_np.stack([(pair >= s) & (pair < 2 * s) for s in sizes], axis=1)
                                            .astype(_np.uint32)))
    add("ada_sel_dram", _np.array([[1, 0], [1, 0], [0, 1], [0, 1], [1, 1]], dtype=_np.float32))
    shape = (1, 256, 2048)
    args.append(nc.dram_tensor("out_dram", shape, F32, kind="ExternalOutput").ap())
    bass_hgrn2_gla_block(nc, *args)
    r = _run(nc, [arrays], core_ids=[0])
    return r.results[0]["out_dram"]
```
